# Optimizing a Trainium2 kernel written in Bass

```python
import math
import jax
import jax.numpy as jnp
from jax import lax
import numpy as np
import jax, jax.numpy as jnp

D_MODEL = 1024
BATCH = 1
SEQ = 256
DEPTH = 2

CHUNK = 64
Q_BLOCK = 128
NORM_EPS = 1e-6
NEG_INF = -1e30

N_EVEN = (DEPTH + 1) // 2
N_ODD = DEPTH // 2

RWKV_HEAD_DIM = 64
RWKV_WIDTH = D_MODEL // 2
RWKV_HEADS = RWKV_WIDTH // RWKV_HEAD_DIM
DECAY_LORA = 64
ICLR_LORA = 64
GATE_LORA = 160
RWKV_GN_EPS = 1e-5 * RWKV_HEAD_DIM
RWKV_SPLITS = (RWKV_WIDTH, 2 * RWKV_WIDTH, 3 * RWKV_WIDTH,
               3 * RWKV_WIDTH + DECAY_LORA, 3 * RWKV_WIDTH + DECAY_LORA + ICLR_LORA)
RWKV_COLS = 3 * RWKV_WIDTH + DECAY_LORA + ICLR_LORA + GATE_LORA

S5_WIDTH = D_MODEL - RWKV_WIDTH
S5_GROUP = 16
S5_GROUPS = S5_WIDTH // S5_GROUP
S5_STATE = 64
S5_DT_MIN = 1e-3
S5_DT_MAX = 1e-1

IN_COLS = RWKV_COLS + S5_WIDTH
MIX_WIDTH = RWKV_WIDTH + S5_WIDTH

DIFF_HEAD_DIM = 64
DIFF_V_DIM = 2 * DIFF_HEAD_DIM
DIFF_HEADS = D_MODEL // DIFF_V_DIM
DIFF_WIDTH = DIFF_HEADS * DIFF_V_DIM

MEM_LEN = 256
MEM_HEADS = 4
MEM_HEAD_DIM = D_MODEL // MEM_HEADS

D_FF = 2816
N_EXPERTS = 8
TOP_K = 2
D_FF_EXPERT = 3584


F32 = jnp.float32

def rms_norm(x, gain):
    xf = x.astype(F32)
    y = xf * lax.rsqrt(jnp.mean(xf * xf, axis=-1, keepdims=True) + NORM_EPS)
    return (y * gain.astype(F32)).astype(x.dtype)

def token_shift(z):
    return jnp.pad(z, ((0, 0), (1, 0), (0, 0)))[:, :-1]

def alibi_slopes(n_heads):
    return 2.0 ** (-8.0 * jnp.arange(1, n_heads + 1, dtype=F32) / n_heads)

def rwkv7_recurrence(r, decay, k, v, kk, a):
    b, _, h, n = r.shape

    def step(state, inp):
        r_t, w_t, k_t, v_t, kk_t, a_t = inp
        s_kk = jnp.einsum('bhvk,bhk->bhv', state, kk_t)
        state = (state * w_t[:, :, None, :]
                 - s_kk[..., None] * (kk_t * a_t)[:, :, None, :]
                 + v_t[..., None] * k_t[:, :, None, :])
        return state, jnp.einsum('bhvk,bhk->bhv', state, r_t)

    xs = tuple(jnp.moveaxis(t, 1, 0) for t in (r, decay, k, v, kk, a))
    _, out = lax.scan(step, jnp.zeros((b, h, n, n), F32), xs)
    return jnp.moveaxis(out, 0, 1)

def rwkv7_time_mix(zr, mu, w0, w_up, a0, a_up, g_up, k_k, k_a, r_k, ln_w, ln_b):
    b, t, _ = zr.shape
    zr = zr.astype(F32)
    zr = zr + (token_shift(zr) - zr) * mu.astype(F32)
    r, k, v, wd, ad, gd = jnp.split(zr, RWKV_SPLITS, axis=-1)
    heads = lambda u: u.reshape(b, t, RWKV_HEADS, RWKV_HEAD_DIM)
    w_log = -jax.nn.softplus(-(w0.astype(F32) + jnp.tanh(wd) @ w_up.astype(F32))) - 0.5
    decay = jnp.exp(-jnp.exp(w_log))
    a = jax.nn.sigmoid(a0.astype(F32) + ad @ a_up.astype(F32))
    g = jax.nn.sigmoid(gd) @ g_up.astype(F32)
    kk = heads(k * k_k.astype(F32))
    kk = kk * lax.rsqrt(jnp.maximum(jnp.sum(kk * kk, axis=-1, keepdims=True), 1e-24))
    k = k * (1.0 + (a - 1.0) * k_a.astype(F32))
    r_h, k_h, v_h = heads(r), heads(k), heads(v)
    o = rwkv7_recurrence(r_h, heads(decay), k_h, v_h, kk, heads(a))
    mean = jnp.mean(o, axis=-1, keepdims=True)
    var = jnp.mean(jnp.square(o - mean), axis=-1, keepdims=True)
    o = ((o - mean) * lax.rsqrt(var + RWKV_GN_EPS)).reshape(b, t, RWKV_WIDTH)
    o = o * ln_w.astype(F32) + ln_b.astype(F32)
    bonus = jnp.sum(r_h * k_h * r_k.astype(F32), axis=-1, keepdims=True) * v_h
    return (o + bonus.reshape(b, t, RWKV_WIDTH)) * g

def s5_ssm(u, lam_re, lam_im, log_dt, b_re, b_im, c_re, c_im, d_skip, w_glu, b_glu):
    b, t, _ = u.shape
    ug = u.astype(F32).reshape(b, t, S5_GROUPS, S5_GROUP)
    lam = lax.complex(lam_re.astype(F32), lam_im.astype(F32))
    dt = jnp.exp(log_dt.astype(F32))[:, None]
    lam_bar = jnp.exp(lam * dt)
    b_bar = ((lam_bar - 1.0) / lam)[..., None] * lax.complex(b_re.astype(F32), b_im.astype(F32))
    bu = jnp.einsum('gpi,btgi->btgp', b_bar, ug.astype(jnp.complex64))

    def combine(left, right):
        a_l, x_l = left
        a_r, x_r = right
        return a_r * a_l, a_r * x_l + x_r

    _, states = lax.associative_scan(combine, (jnp.broadcast_to(lam_bar, bu.shape), bu), axis=1)
    c_mat = lax.complex(c_re.astype(F32), c_im.astype(F32))
    y = jnp.real(jnp.einsum('gip,btgp->btgi', c_mat, states))
    y = y + d_skip.astype(F32).reshape(S5_GROUPS, S5_GROUP) * ug
    y = jax.nn.gelu(y.reshape(b, t, S5_WIDTH))
    return y * jax.nn.sigmoid(y @ w_glu.astype(F32) + b_glu.astype(F32))

def diff_attention(h, w_qkv, q_gain, k_gain, lam_q1, lam_k1, lam_q2, lam_k2, sub_gain, w_o, lambda_init):
    b, t, _ = h.shape
    q, k, v = jnp.split(h @ w_qkv, 3, axis=-1)
    q = rms_norm(q.reshape(b, t, DIFF_HEADS, 2, DIFF_HEAD_DIM), q_gain).astype(F32)
    k = rms_norm(k.reshape(b, t, DIFF_HEADS, 2, DIFF_HEAD_DIM), k_gain).astype(F32)
    v = v.reshape(b, t, DIFF_HEADS, DIFF_V_DIM).astype(F32)
    lam = (jnp.exp(jnp.sum(lam_q1.astype(F32) * lam_k1.astype(F32)))
           - jnp.exp(jnp.sum(lam_q2.astype(F32) * lam_k2.astype(F32))) + lambda_init)
    slopes = alibi_slopes(DIFF_HEADS)
    key_pos = jnp.arange(t)
    n_blocks = t // Q_BLOCK
    q_blocks = jnp.moveaxis(q.reshape(b, n_blocks, Q_BLOCK, DIFF_HEADS, 2, DIFF_HEAD_DIM), 1, 0)
    starts = jnp.arange(n_blocks) * Q_BLOCK
    scale = DIFF_HEAD_DIM ** -0.5

    def attend_block(args):
        qb, start = args
        q_pos = start + jnp.arange(Q_BLOCK)
        s = jnp.einsum('bqhcd,bshcd->bhcqs', qb, k) * scale
        dist = jnp.abs(q_pos[:, None] - key_pos[None, :]).astype(F32)
        bias = -slopes[:, None, None, None] * dist
        visible = (key_pos[None, :] // CHUNK) <= (q_pos[:, None] // CHUNK)
        p = jax.nn.softmax(jnp.where(visible, s + bias, NEG_INF), axis=-1)
        attn = p[:, :, 0] - lam * p[:, :, 1]
        return jnp.einsum('bhqs,bshe->bqhe', attn, v)

    o = lax.map(attend_block, (q_blocks, starts))
    o = jnp.moveaxis(o, 0, 1).reshape(b, t, DIFF_HEADS, DIFF_V_DIM)
    o = rms_norm(o, sub_gain) * (1.0 - lambda_init)
    return o.reshape(b, t, DIFF_WIDTH).astype(h.dtype) @ w_o

def memory_cross_attention(h, mem_n, w_q, w_kv, q_gain, k_gain, w_o):
    b, t, _ = h.shape
    m = mem_n.shape[1]
    q = rms_norm((h @ w_q).reshape(b, t, MEM_HEADS, MEM_HEAD_DIM), q_gain).astype(F32)
    k, v = jnp.split(mem_n @ w_kv, 2, axis=-1)
    k = rms_norm(k.reshape(b, m, MEM_HEADS, MEM_HEAD_DIM), k_gain).astype(F32)
    v = v.reshape(b, m, MEM_HEADS, MEM_HEAD_DIM).astype(F32)
    p = jax.nn.softmax(jnp.einsum('bthd,bmhd->bhtm', q, k) * MEM_HEAD_DIM ** -0.5, axis=-1)
    o = jnp.einsum('bhtm,bmhd->bthd', p, v).reshape(b, t, D_MODEL)
    return o.astype(h.dtype) @ w_o

def swiglu(h, w_gate, w_up, w_down):
    return (jax.nn.silu(h @ w_gate) * (h @ w_up)) @ w_down

def moe_swiglu(h, w_router, b_router, w_gate, w_up, w_down):
    logits = (h @ w_router).astype(F32) + b_router.astype(F32)
    top_logits, top_idx = lax.top_k(logits, TOP_K)
    top_w = jax.nn.softmax(top_logits, axis=-1)
    gates = jnp.sum(jax.nn.one_hot(top_idx, N_EXPERTS, dtype=F32) * top_w[..., None], axis=-2)
    out = jnp.zeros(h.shape, F32)
    for e in range(N_EXPERTS):
        y_e = swiglu(h, w_gate[e], w_up[e], w_down[e]).astype(F32)
        out = out + gates[..., e:e + 1] * y_e
    return out.astype(h.dtype)

def first_inputs(seed: int = 0) -> dict:
    key = jax.random.key(seed)
    keys = iter(jax.random.split(key, 80))

    def nrm(shape, scale):
        return jax.random.normal(next(keys), shape, F32) * scale

    def gain(shape):
        return 1.0 + nrm(shape, 0.02)

    D, L, NE, NO = D_MODEL, DEPTH, N_EVEN, N_ODD
    G, P, I = S5_GROUPS, S5_STATE, S5_GROUP
    decay_ramp = -6.5 + 5.0 * jnp.linspace(0.0, 1.0, RWKV_WIDTH, dtype=F32) ** 0.85
    return {
        'x': nrm((BATCH, SEQ, D), 1.0),
        'mem': nrm((BATCH, MEM_LEN, D), 1.0),
        'norm_mix': gain((L, D)),
        'norm_xattn': gain((L, D)),
        'norm_mem': gain((L, D)),
        'norm_ffn': gain((L, D)),
        'xa_w_q': nrm((L, D, D), D ** -0.5),
        'xa_w_kv': nrm((L, D, 2 * D), D ** -0.5),
        'xa_q_gain': gain((L, MEM_HEAD_DIM)),
        'xa_k_gain': gain((L, MEM_HEAD_DIM)),
        'xa_w_o': nrm((L, D, D), D ** -0.5),
        'hy_w_in': nrm((NE, D, IN_COLS), D ** -0.5),
        'rw_mu': jax.random.uniform(next(keys), (NE, RWKV_COLS), F32),
        'rw_w0': decay_ramp + nrm((NE, RWKV_WIDTH), 0.01),
        'rw_w_up': nrm((NE, DECAY_LORA, RWKV_WIDTH), 0.1),
        'rw_a0': nrm((NE, RWKV_WIDTH), 0.1),
        'rw_a_up': nrm((NE, ICLR_LORA, RWKV_WIDTH), ICLR_LORA ** -0.5),
        'rw_g_up': nrm((NE, GATE_LORA, RWKV_WIDTH), GATE_LORA ** -0.5),
        'rw_k_k': 0.85 + nrm((NE, RWKV_WIDTH), 0.02),
        'rw_k_a': gain((NE, RWKV_WIDTH)),
        'rw_r_k': nrm((NE, RWKV_HEADS, RWKV_HEAD_DIM), 0.1),
        'rw_ln_w': gain((NE, RWKV_WIDTH)),
        'rw_ln_b': nrm((NE, RWKV_WIDTH), 0.02),
        's5_lam_re': -0.5 + nrm((NE, G, P), 0.01),
        's5_lam_im': jnp.pi * jnp.arange(P, dtype=F32) + nrm((NE, G, P), 0.01),
        's5_log_dt': jax.random.uniform(next(keys), (NE, G), F32, math.log(S5_DT_MIN), math.log(S5_DT_MAX)),
        's5_b_re': nrm((NE, G, P, I), (2 * I) ** -0.5),
        's5_b_im': nrm((NE, G, P, I), (2 * I) ** -0.5),
        's5_c_re': nrm((NE, G, I, P), P ** -0.5),
        's5_c_im': nrm((NE, G, I, P), P ** -0.5),
        's5_d': nrm((NE, S5_WIDTH), 1.0),
        's5_w_glu': nrm((NE, S5_WIDTH, S5_WIDTH), S5_WIDTH ** -0.5),
        's5_b_glu': nrm((NE, S5_WIDTH), 0.02),
        'hy_w_out': nrm((NE, MIX_WIDTH, D), MIX_WIDTH ** -0.5),
        'ff_w_gate': nrm((NE, D, D_FF), D ** -0.5),
        'ff_w_up': nrm((NE, D, D_FF), D ** -0.5),
        'ff_w_down': nrm((NE, D_FF, D), D_FF ** -0.5),
        'da_w_qkv': nrm((NO, D, 3 * DIFF_WIDTH), D ** -0.5),
        'da_q_gain': gain((NO, DIFF_HEAD_DIM)),
        'da_k_gain': gain((NO, DIFF_HEAD_DIM)),
        'da_lam_q1': nrm((NO, DIFF_HEAD_DIM), 0.1),
        'da_lam_k1': nrm((NO, DIFF_HEAD_DIM), 0.1),
        'da_lam_q2': nrm((NO, DIFF_HEAD_DIM), 0.1),
        'da_lam_k2': nrm((NO, DIFF_HEAD_DIM), 0.1),
        'da_sub_gain': gain((NO, DIFF_V_DIM)),
        'da_w_o': nrm((NO, DIFF_WIDTH, D), DIFF_WIDTH ** -0.5),
        'moe_w_router': nrm((NO, D, N_EXPERTS), D ** -0.5),
        'moe_b_router': nrm((NO, N_EXPERTS), 0.01),
        'moe_w_gate': nrm((NO, N_EXPERTS, D, D_FF_EXPERT), D ** -0.5),
        'moe_w_up': nrm((NO, N_EXPERTS, D, D_FF_EXPERT), D ** -0.5),
        'moe_w_down': nrm((NO, N_EXPERTS, D_FF_EXPERT, D), D_FF_EXPERT ** -0.5),
    }

def first_block(x, mem, norm_mix, norm_xattn, norm_mem, norm_ffn,
              xa_w_q, xa_w_kv, xa_q_gain, xa_k_gain, xa_w_o,
              hy_w_in, rw_mu, rw_w0, rw_w_up, rw_a0, rw_a_up, rw_g_up, rw_k_k, rw_k_a, rw_r_k,
              rw_ln_w, rw_ln_b,
              s5_lam_re, s5_lam_im, s5_log_dt, s5_b_re, s5_b_im, s5_c_re, s5_c_im, s5_d,
              s5_w_glu, s5_b_glu, hy_w_out,
              ff_w_gate, ff_w_up, ff_w_down,
              da_w_qkv, da_q_gain, da_k_gain, da_lam_q1, da_lam_k1, da_lam_q2, da_lam_k2,
              da_sub_gain, da_w_o,
              moe_w_router, moe_b_router, moe_w_gate, moe_w_up, moe_w_down):
    h = x
    for l in range(DEPTH):
        i = l // 2
        hn = rms_norm(h, norm_mix[l])
        if l % 2 == 0:
            z = hn @ hy_w_in[i]
            y_a = rwkv7_time_mix(z[..., :RWKV_COLS], rw_mu[i], rw_w0[i], rw_w_up[i], rw_a0[i],
                                 rw_a_up[i], rw_g_up[i], rw_k_k[i], rw_k_a[i], rw_r_k[i],
                                 rw_ln_w[i], rw_ln_b[i])
            y_b = s5_ssm(z[..., RWKV_COLS:], s5_lam_re[i], s5_lam_im[i], s5_log_dt[i], s5_b_re[i],
                         s5_b_im[i], s5_c_re[i], s5_c_im[i], s5_d[i], s5_w_glu[i], s5_b_glu[i])
            y_mix = jnp.concatenate([y_a, y_b], axis=-1).astype(h.dtype) @ hy_w_out[i]
        else:
            lambda_init = 0.8 - 0.6 * math.exp(-0.3 * l)
            y_mix = diff_attention(hn, da_w_qkv[i], da_q_gain[i], da_k_gain[i], da_lam_q1[i],
                                   da_lam_k1[i], da_lam_q2[i], da_lam_k2[i], da_sub_gain[i],
                                   da_w_o[i], lambda_init)
        h = h + y_mix.astype(h.dtype)
        y_mem = memory_cross_attention(rms_norm(h, norm_xattn[l]), rms_norm(mem, norm_mem[l]),
                                       xa_w_q[l], xa_w_kv[l], xa_q_gain[l], xa_k_gain[l], xa_w_o[l])
        h = h + y_mem.astype(h.dtype)
        hn = rms_norm(h, norm_ffn[l])
        if l % 2 == 0:
            y_ff = swiglu(hn, ff_w_gate[i], ff_w_up[i], ff_w_down[i])
        else:
            y_ff = moe_swiglu(hn, moe_w_router[i], moe_b_router[i], moe_w_gate[i],
                              moe_w_up[i], moe_w_down[i])
        h = h + y_ff.astype(h.dtype)
    return h


HEAD_DIM = 64
N_HEADS_MOBA = 6
N_HEADS_MLA = 4
N_HEADS_FOX = 6
MOBA_BLOCK = 256
MOBA_TOPK = 3
MOBA_Q_BLOCK = 32
MLA_Q_RANK = 256
MLA_KV_RANK = 128
MLA_NOPE_DIM = 64
MLA_ROPE_DIM = 32
MLA_V_DIM = 64
MLA_QK_DIM = MLA_NOPE_DIM + MLA_ROPE_DIM
ROPE_THETA = 10000.0
T5_BUCKETS = 32
T5_MAX_DIST = 1024
CONV_WIDTH = 3
NEG_INF_2 = -1e30

W_MOBA = N_HEADS_MOBA * HEAD_DIM
W_MLA = N_HEADS_MLA * MLA_V_DIM
W_FOX = N_HEADS_FOX * HEAD_DIM
MIX_WIDTH_2 = W_MOBA + W_MLA + W_FOX
PROJ_SIZES = (W_MOBA, W_MOBA, W_MOBA, MLA_Q_RANK, MLA_KV_RANK, MLA_ROPE_DIM, W_FOX, W_FOX, W_FOX, N_HEADS_FOX)
PROJ_COLS = sum(PROJ_SIZES)


def rms_norm_2(x, g):
    xf = x.astype(jnp.float32)
    y = xf * lax.rsqrt(jnp.mean(xf * xf, axis=-1, keepdims=True) + NORM_EPS)
    return (y * g.astype(jnp.float32)).astype(x.dtype)

def split_heads(t, n, d):
    b, s, _ = t.shape
    return t.reshape(b, s, n, d).transpose(0, 2, 1, 3)

def merge_heads(t):
    b, h, s, d = t.shape
    return t.transpose(0, 2, 1, 3).reshape(b, s, h * d)

def rotary(t, pos):
    half = t.shape[-1] // 2
    inv = ROPE_THETA ** (-jnp.arange(half, dtype=jnp.float32) / half)
    ang = pos.astype(jnp.float32)[:, None] * inv[None, :]
    cos, sin = jnp.cos(ang), jnp.sin(ang)
    t1 = t[..., :half].astype(jnp.float32)
    t2 = t[..., half:].astype(jnp.float32)
    return jnp.concatenate([t1 * cos - t2 * sin, t1 * sin + t2 * cos], axis=-1).astype(t.dtype)

def t5_bucket(rel):
    n = jnp.maximum(rel, 0)
    exact = T5_BUCKETS // 2
    large = exact + (jnp.log(jnp.maximum(n, 1).astype(jnp.float32) / exact)
                     / math.log(T5_MAX_DIST / exact) * (T5_BUCKETS - exact)).astype(jnp.int32)
    return jnp.where(n < exact, n, jnp.minimum(large, T5_BUCKETS - 1))

def moba_attention(q, k, v, rel_bias):
    b, h, s, dh = q.shape
    nb = -(-s // MOBA_BLOCK)
    pad = nb * MOBA_BLOCK - s
    kp = jnp.pad(k, ((0, 0), (0, 0), (0, pad), (0, 0)))
    vp = jnp.pad(v, ((0, 0), (0, 0), (0, pad), (0, 0)))
    k_blocks = kp.reshape(b, h, nb, MOBA_BLOCK, dh)
    v_blocks = vp.reshape(b, h, nb, MOBA_BLOCK, dh)
    k_mean = jnp.mean(k_blocks, axis=3)
    topk = min(MOBA_TOPK, nb)
    bias_tab = rel_bias.T
    scale = dh ** -0.5
    b_idx = jnp.arange(b)[:, None, None, None]
    h_idx = jnp.arange(h)[None, :, None, None]
    blk_pos = jnp.arange(MOBA_BLOCK)

    def chunk(c):
        q_start = c * MOBA_Q_BLOCK
        qc = lax.dynamic_slice_in_dim(q, q_start, MOBA_Q_BLOCK, axis=2)
        q_pos = q_start + jnp.arange(MOBA_Q_BLOCK)
        own = q_start // MOBA_BLOCK
        gate = jnp.einsum('bhqd,bhnd->bhqn', qc, k_mean).astype(jnp.float32)
        gate = jnp.where(jnp.arange(nb) < own, gate, NEG_INF_2)
        _, sel = lax.top_k(gate, topk)
        valid = jnp.arange(topk) < own
        k_sel = k_blocks[b_idx, h_idx, sel]
        v_sel = v_blocks[b_idx, h_idx, sel]
        k_pos_sel = sel[..., None] * MOBA_BLOCK + blk_pos
        s_sel = jnp.einsum('bhqd,bhqnkd->bhqnk', qc, k_sel).astype(jnp.float32) * scale
        s_sel = s_sel + bias_tab[h_idx[..., None], t5_bucket(q_pos[:, None, None] - k_pos_sel)]
        s_sel = jnp.where(valid[:, None], s_sel, NEG_INF_2)
        s_sel = s_sel.reshape(b, h, MOBA_Q_BLOCK, topk * MOBA_BLOCK)
        own_start = own * MOBA_BLOCK
        k_own = lax.dynamic_slice_in_dim(kp, own_start, MOBA_BLOCK, axis=2)
        v_own = lax.dynamic_slice_in_dim(vp, own_start, MOBA_BLOCK, axis=2)
        rel = q_pos[:, None] - (own_start + blk_pos)[None, :]
        s_own = jnp.einsum('bhqd,bhkd->bhqk', qc, k_own).astype(jnp.float32) * scale
        s_own = jnp.where(rel >= 0, s_own + bias_tab[:, t5_bucket(rel)], NEG_INF_2)
        p = jax.nn.softmax(jnp.concatenate([s_sel, s_own], axis=-1), axis=-1).astype(v.dtype)
        p_sel = p[..., :topk * MOBA_BLOCK].reshape(b, h, MOBA_Q_BLOCK, topk, MOBA_BLOCK)
        p_own = p[..., topk * MOBA_BLOCK:]
        return (jnp.einsum('bhqnk,bhqnkd->bhqd', p_sel, v_sel)
                + jnp.einsum('bhqk,bhkd->bhqd', p_own, v_own))

    outs = lax.map(chunk, jnp.arange(s // MOBA_Q_BLOCK))
    return outs.transpose(1, 2, 0, 3, 4).reshape(b, h, s, dh)

def causal_block_attention(q, k, v, scale, decay=None):
    b, h, s, _ = q.shape
    dv = v.shape[-1]
    k_pos = jnp.arange(s)

    def chunk(c):
        q_start = c * Q_BLOCK
        qc = lax.dynamic_slice_in_dim(q, q_start, Q_BLOCK, axis=2)
        q_pos = q_start + jnp.arange(Q_BLOCK)
        sc = jnp.einsum('bhqd,bhkd->bhqk', qc, k).astype(jnp.float32) * scale
        if decay is not None:
            dq = lax.dynamic_slice_in_dim(decay, q_start, Q_BLOCK, axis=2)
            sc = sc + dq[..., None] - decay[:, :, None, :]
        sc = jnp.where(k_pos[None, :] <= q_pos[:, None], sc, NEG_INF_2)
        p = jax.nn.softmax(sc, axis=-1).astype(v.dtype)
        return jnp.einsum('bhqk,bhkd->bhqd', p, v)

    outs = lax.map(chunk, jnp.arange(s // Q_BLOCK))
    return outs.transpose(1, 2, 0, 3, 4).reshape(b, h, s, dv)

def hybrid_mixer(h, rel_bias, w_in, b_f, q_norm, kv_norm, w_uq, w_ukv, w_o):
    b, s, _ = h.shape
    pos = jnp.arange(s)
    proj = h @ w_in
    (a_q, a_k, a_v, c_q, c_kv, k_r, f_q, f_k, f_v, f_g) = jnp.split(
        proj, np.cumsum(PROJ_SIZES)[:-1].tolist(), axis=-1)

    out_a = moba_attention(split_heads(a_q, N_HEADS_MOBA, HEAD_DIM),
                           split_heads(a_k, N_HEADS_MOBA, HEAD_DIM),
                           split_heads(a_v, N_HEADS_MOBA, HEAD_DIM), rel_bias)

    qb = split_heads(rms_norm_2(c_q, q_norm) @ w_uq, N_HEADS_MLA, MLA_QK_DIM)
    kv = split_heads(rms_norm_2(c_kv, kv_norm) @ w_ukv, N_HEADS_MLA, MLA_NOPE_DIM + MLA_V_DIM)
    k_nope, v_b = kv[..., :MLA_NOPE_DIM], kv[..., MLA_NOPE_DIM:]
    q_b = jnp.concatenate([qb[..., :MLA_NOPE_DIM], rotary(qb[..., MLA_NOPE_DIM:], pos)], axis=-1)
    k_rope = jnp.broadcast_to(rotary(k_r[:, None], pos), (b, N_HEADS_MLA, s, MLA_ROPE_DIM))
    k_b = jnp.concatenate([k_nope, k_rope], axis=-1)
    out_b = causal_block_attention(q_b, k_b, v_b, MLA_QK_DIM ** -0.5)

    log_f = jax.nn.log_sigmoid(f_g.astype(jnp.float32) + b_f.astype(jnp.float32))
    decay = jnp.cumsum(log_f, axis=1).transpose(0, 2, 1)
    out_c = causal_block_attention(split_heads(f_q, N_HEADS_FOX, HEAD_DIM),
                                   split_heads(f_k, N_HEADS_FOX, HEAD_DIM),
                                   split_heads(f_v, N_HEADS_FOX, HEAD_DIM),
                                   HEAD_DIM ** -0.5, decay)

    merged = jnp.concatenate([merge_heads(out_a), merge_heads(out_b), merge_heads(out_c)], axis=-1)
    return merged @ w_o

def conv_ffn(h, w_up, conv_w, conv_b, w_down):
    u = h @ w_up
    u = lax.conv_general_dilated(u, conv_w[:, None, :], window_strides=(1,),
                                 padding=[(CONV_WIDTH - 1, 0)],
                                 dimension_numbers=('NWC', 'WIO', 'NWC'),
                                 feature_group_count=u.shape[-1]) + conv_b
    g, val = jnp.split(u, 2, axis=-1)
    return (jax.nn.gelu(g, approximate=True) * val) @ w_down

def second_inputs(seed: int = 0) -> dict:
    key = jax.random.key(seed)
    ks = jax.random.split(key, 20)
    f32 = jnp.float32

    def nrm(k, shape, fan_in):
        return jax.random.normal(k, shape, f32) * (fan_in ** -0.5)

    def gain(k, shape):
        return 1.0 + 0.1 * jax.random.normal(k, shape, f32)

    L = DEPTH
    return {
        "x": jax.random.normal(ks[0], (BATCH, SEQ, D_MODEL), f32),
        "rel_bias": 0.5 * jax.random.normal(ks[1], (T5_BUCKETS, N_HEADS_MOBA), f32),
        "ln_mix_pre": gain(ks[2], (L, D_MODEL)),
        "ln_mix_post": gain(ks[3], (L, D_MODEL)),
        "ln_ffn_pre": gain(ks[4], (L, D_MODEL)),
        "ln_ffn_post": gain(ks[5], (L, D_MODEL)),
        "w_in": nrm(ks[6], (L, D_MODEL, PROJ_COLS), D_MODEL),
        "b_f": 2.0 + 0.5 * jax.random.normal(ks[7], (L, N_HEADS_FOX), f32),
        "q_norm": gain(ks[8], (L, MLA_Q_RANK)),
        "kv_norm": gain(ks[9], (L, MLA_KV_RANK)),
        "w_uq": nrm(ks[10], (L, MLA_Q_RANK, N_HEADS_MLA * MLA_QK_DIM), MLA_Q_RANK),
        "w_ukv": nrm(ks[11], (L, MLA_KV_RANK, N_HEADS_MLA * (MLA_NOPE_DIM + MLA_V_DIM)), MLA_KV_RANK),
        "w_o": nrm(ks[12], (L, MIX_WIDTH_2, D_MODEL), MIX_WIDTH_2),
        "w_up": nrm(ks[13], (L, D_MODEL, 2 * D_FF), D_MODEL),
        "conv_w": nrm(ks[14], (L, CONV_WIDTH, 2 * D_FF), CONV_WIDTH),
        "conv_b": 0.01 * jax.random.normal(ks[15], (L, 2 * D_FF), f32),
        "w_down": nrm(ks[16], (L, D_FF, D_MODEL), D_FF),
    }

def second_block(x, rel_bias, ln_mix_pre, ln_mix_post, ln_ffn_pre, ln_ffn_post, w_in, b_f,
              q_norm, kv_norm, w_uq, w_ukv, w_o, w_up, conv_w, conv_b, w_down):
    for l in range(DEPTH):
        h = rms_norm_2(x, ln_mix_pre[l])
        x = x + rms_norm_2(hybrid_mixer(h, rel_bias, w_in[l], b_f[l], q_norm[l], kv_norm[l],
                                      w_uq[l], w_ukv[l], w_o[l]), ln_mix_post[l])
        h = rms_norm_2(x, ln_ffn_pre[l])
        x = x + rms_norm_2(conv_ffn(h, w_up[l], conv_w[l], conv_b[l], w_down[l]), ln_ffn_post[l])
    return x


def setup_inputs(seed=0):
    out = dict(first_inputs(seed))
    for name, value in second_inputs(seed + 1).items():
        if name != "x":
            out[name + "_2"] = value
    return out


def reference(
    x, mem, norm_mix, norm_xattn, norm_mem, norm_ffn, xa_w_q, xa_w_kv, xa_q_gain, xa_k_gain,
    xa_w_o, hy_w_in, rw_mu, rw_w0, rw_w_up, rw_a0, rw_a_up, rw_g_up, rw_k_k, rw_k_a, rw_r_k,
    rw_ln_w, rw_ln_b, s5_lam_re, s5_lam_im, s5_log_dt, s5_b_re, s5_b_im, s5_c_re, s5_c_im, s5_d,
    s5_w_glu, s5_b_glu, hy_w_out, ff_w_gate, ff_w_up, ff_w_down, da_w_qkv, da_q_gain, da_k_gain,
    da_lam_q1, da_lam_k1, da_lam_q2, da_lam_k2, da_sub_gain, da_w_o, moe_w_router, moe_b_router,
    moe_w_gate, moe_w_up, moe_w_down, rel_bias_2, ln_mix_pre_2, ln_mix_post_2, ln_ffn_pre_2,
    ln_ffn_post_2, w_in_2, b_f_2, q_norm_2, kv_norm_2, w_uq_2, w_ukv_2, w_o_2, w_up_2, conv_w_2,
    conv_b_2, w_down_2,
):
    x = first_block(
        x, mem, norm_mix, norm_xattn, norm_mem, norm_ffn, xa_w_q, xa_w_kv, xa_q_gain, xa_k_gain,
        xa_w_o, hy_w_in, rw_mu, rw_w0, rw_w_up, rw_a0, rw_a_up, rw_g_up, rw_k_k, rw_k_a, rw_r_k,
        rw_ln_w, rw_ln_b, s5_lam_re, s5_lam_im, s5_log_dt, s5_b_re, s5_b_im, s5_c_re, s5_c_im,
        s5_d, s5_w_glu, s5_b_glu, hy_w_out, ff_w_gate, ff_w_up, ff_w_down, da_w_qkv, da_q_gain,
        da_k_gain, da_lam_q1, da_lam_k1, da_lam_q2, da_lam_k2, da_sub_gain, da_w_o,
        moe_w_router, moe_b_router, moe_w_gate, moe_w_up, moe_w_down,
    )
    return second_block(
        x, rel_bias_2, ln_mix_pre_2, ln_mix_post_2, ln_ffn_pre_2, ln_ffn_post_2, w_in_2, b_f_2,
        q_norm_2, kv_norm_2, w_uq_2, w_ukv_2, w_o_2, w_up_2, conv_w_2, conv_b_2, w_down_2,
    )


_drawn_inputs = setup_inputs


def setup_inputs(seed=0):
    import zlib

    import numpy as np

    out = dict(_drawn_inputs(seed))
    spreads = {}
    factors = {'norm_xattn': 4.277,
     'norm_mem': 3.4,
     'xa_q_gain': 3.645,
     'xa_k_gain': 3.684,
     'rw_k_k': 7.463,
     's5_lam_re': 200.0,
     's5_b_glu': 2.719,
     'da_lam_q1': 25.817,
     'q_norm_2': 3.664,
     'conv_b_2': 5.832,
     'da_q_gain': 4.366,
     'da_k_gain': 4.727,
     'da_lam_k2': 4.632,
     'da_sub_gain': 4.121,
     'moe_b_router': 16.68}
    for name, (base, spread) in spreads.items():
        noise = np.random.default_rng([zlib.crc32(name.encode()), seed]).standard_normal(out[name].shape)
        drawn = base * np.exp(spread * noise) if base else spread * noise
        out[name] = jnp.asarray(drawn.astype(out[name].dtype))
    for name, factor in factors.items():
        out[name] = (out[name] * factor).astype(out[name].dtype)
    return out
```

```python
from contextlib import ExitStack

import numpy as np

import concourse.bass as bass
from concourse import mybir

F32 = mybir.dt.float32
ALU = mybir.AluOpType
ACT = mybir.ActivationFunctionType
AX_X = mybir.AxisListType.X

P = 128
T = 256
TT = T // P
D = 1024
DT = D // P
EPS = 1e-6
LAMBDA_INIT = 0.8 - 0.6 * float(np.exp(-0.3))
RING = 7
CHUNK = 2048
D_FF = 2816
FT = D_FF // P
N_EXPERTS = 8
D_FE = 3584
ET = D_FE // P
RW = 512
NCH = T // 64
MASKED = -1e30
CROWD = P
LN2 = float(np.log(2.0))


def const_arrays():
    f = np.float32
    i = np.arange(P)
    c = {}
    c["ident"] = np.eye(P, dtype=f)
    c["half_ones"] = (i[:, None] // 64 == i[None, :] // 64).astype(f)
    causal = np.zeros((P, T), f)
    causal[:, P:] = np.where(i[None, :] <= i[:, None], 0.0, MASKED)
    c["causal"] = causal
    key, query = np.arange(T), P + i
    far = np.abs(query[:, None] - key[None, :]).astype(f)
    c["distance"] = np.where(key[None, :] // 64 <= query[:, None] // 64, far, 1e33).astype(f)
    c["before"] = (i[:, None] < i[None, :]).astype(f)
    c["flip"] = np.eye(P, dtype=f)[::-1].copy()
    c["slots"] = np.tile(np.arange(T, dtype=f), (P, 1))
    s = np.arange(64)
    strict = (s[:, None] < s[None, :]).astype(f)
    upto = (s[:, None] <= s[None, :]).astype(f)
    rows = [strict, upto, strict, -upto]
    for m in (1, 2, 4, 8, 16, 32):
        low = ((s[:, None] // (2 * m) == s[None, :] // (2 * m)) & (s[:, None] % (2 * m) >= m)
               & (s[None, :] % (2 * m) < m)).astype(f)
        rows += [low.T] if m > 1 else [-low, -low.T]
    rows.append(np.eye(64, dtype=f))
    c["chunk_masks"] = np.concatenate(rows, 1)
    half = 16
    inv = (f(10000.0) ** (-np.arange(half, dtype=f) / f(half))).astype(f)
    ang = np.arange(T, dtype=f)[None, :] * inv[:, None]
    cos, sin = np.ones((96, T), f), np.zeros((96, T), f)
    cos[64:80] = cos[80:96] = np.cos(ang)
    sin[64:80] = sin[80:96] = np.sin(ang)
    swap = np.zeros((96, 96), f)
    for j in range(half):
        swap[80 + j, 64 + j] = -1.0
        swap[64 + j, 80 + j] = 1.0
    c["cos"], c["sin"], c["swap"] = cos, sin, swap
    rel = 255 - np.arange(384)
    n = np.maximum(rel, 0)
    large = 16 + (np.log(np.maximum(n, 1).astype(f) / f(16)) / f(np.log(64.0)) * f(16)).astype(np.int32)
    bucket = np.where(n < 16, n, np.minimum(large, 31))
    c["buckets"] = (np.arange(32)[:, None] == bucket[None, :]).astype(f)
    c["future"] = np.tile(np.where(rel < 0, MASKED, 0.0).astype(f), (6, 1))
    return c


class Signal:

    def __init__(self, sem):
        self.sem, self.base, self.total = sem, 0, 0

    def tick(self, n=1):
        self.total += n
        return n

    def at(self, n):
        return self.base + n


class Chunk:

    def __init__(self, slot, use, src, dst, pos):
        self.slot, self.use, self.src, self.dst, self.pos = slot, use, src, dst, pos
        self.release = None


def build(nc, ins, out, stop):
    with ExitStack() as ctx:
        def sb(name, *shape):
            return ctx.enter_context(nc.sbuf_tensor(name, [P, *shape], F32))

        signals = {}

        def sig(name):
            if name not in signals:
                signals[name] = Signal(ctx.enter_context(nc.semaphore(name)))
            return signals[name]

        h = sb("h", DT, T)
        memn = sb("memn", DT, T)
        ring = sb("ring", RING, CHUNK)
        col = sb("col", 5 * P)
        ident = sb("ident", P)
        ones = sb("ones", P)
        half_ones = sb("half_ones", P)
        misc = sb("misc", 16)
        SCRATCH = 33600
        scratch = sb("scratch", SCRATCH)
        bank = [ctx.enter_context(nc.psum_tensor(f"bank{i}", [P, 512], F32)) for i in range(8)]
        EPS_COL, ZERO_COL, GN_COL, RS_COL, NLAM, ONE_COL, HALFPI = range(7)

        used = [0]

        def take(*shape):
            n = int(np.prod(shape))
            v = scratch[:, used[0]:used[0] + n]
            used[0] += n
            assert used[0] <= SCRATCH, used[0]
            names = " ".join(f"a{k}" for k in range(len(shape)))
            if len(shape) == 1:
                return v
            return v.rearrange(f"p ({names}) -> p {names}", **{f"a{k}": shape[k] for k in range(len(shape))})

        def release(mark=0):
            used[0] = mark

        fence = sig("fence")
        tiles_done = sig("tiles_done")
        landed = [sig(f"landed{i}") for i in range(RING)]
        phases = [0]
        block = ctx.enter_context(nc.Block())

        def end_phase():
            phases[0] += 1
            n = 4 * phases[0]
            for body in (block.tensor, block.vector, block.scalar, block.gpsimd):
                @body
                def _(eng):
                    eng.drain().then_inc(fence.sem, 1)
                    eng.wait_ge(fence.sem, n)
            for s in signals.values():
                s.base = s.total

        plan = []
        slot_use = [0] * RING
        pos = [0]

        def chunk(src, a, b):
            s = pos[0] % RING
            c = Chunk(s, slot_use[s], src, ring[:, s, 0:a * b].rearrange("p (a b) -> p a b", a=a), pos[0])
            slot_use[s] += 1
            pos[0] += 1
            plan.append(c)
            return c

        def col_chunks(w, cuts):
            view = w.rearrange("(k p) n -> p k n", p=P)
            return [chunk(view[:, :, a:b], view.shape[1], b - a) for a, b in zip(cuts, cuts[1:])]

        def row_chunks(w, n=2):
            view = w.rearrange("(k p) n -> p k n", p=P)
            return [chunk(view[:, k:k + n, :], n, w.shape[1]) for k in range(0, view.shape[1], n)]

        def need(pe, c):
            pe.wait_ge(landed[c.slot].sem, 16 * (c.use + 1))

        def stream(pe, tiles, x, nk, free, banks, skip=0):
            marks, seen = [], set()
            for n, (c, a, m) in enumerate(tiles):
                if c.pos not in seen:
                    seen.add(c.pos)
                    need(pe, c)
                if n >= len(banks):
                    pe.wait_ge(free.sem, free.at(skip + n - len(banks) + 1))
                b = banks[n % len(banks)]
                for k in range(nk):
                    mm = pe.matmul(b[0:m, 0:T], c.dst[:, k, a:a + m], x[:, k, :], start=k == 0, stop=k == nk - 1)
                mm.then_inc(tiles_done.sem, tiles_done.tick())
                marks.append(tiles_done.total)
                c.release = tiles_done.total
            return marks

        def ordered(eng, s, ins_):
            ins_.then_inc(s.sem, s.tick())
            eng.wait_ge(s.sem, s.total)

        act_own, dve_own = sig("act_own"), sig("dve_own")

        def colv(name, n=None, off=0):
            a = COLS[name] + off
            return col[:, a:a + (n or 1)]

        COLS = {}
        loads = []
        at = [0]

        def vec(name, src, n, w=P, rep=1):
            COLS[name] = at[0]
            for q in range(rep):
                loads.append((at[0], n, q * w, w, src))
            at[0] += n

        def rows_of(v, w=P):
            return v.rearrange("(k p) -> k p", p=w)

        for name in ("norm_mix", "norm_xattn", "norm_mem", "norm_ffn", "ln_mix_pre_2", "ln_mix_post_2",
                     "ln_ffn_pre_2", "ln_ffn_post_2"):
            vec(name, ins[name].rearrange("l (k p) -> (l k) p", p=P), 16)
        mu = ins["rw_mu"][0]
        vec("mu", rows_of(mu[0:1536]), 12)
        vec("mu_wd", rows_of(mu[1536:1600], 64), 1, 64)
        vec("mu_ad", rows_of(mu[1600:1664], 64), 1, 64)
        vec("mu_gd", rows_of(mu[1664:1792]), 1)
        vec("mu_gd2", rows_of(mu[1792:1824], 32), 1, 32)
        for name in ("rw_w0", "rw_a0", "rw_k_k", "rw_k_a", "rw_ln_w", "rw_ln_b", "s5_d", "s5_b_glu"):
            vec(name, rows_of(ins[name][0]), 4)
        vec("rw_r_k", ins["rw_r_k"][0].rearrange("(k two) p -> k (two p)", two=2), 4)
        vec("q_norm", ins["q_norm_2"].rearrange("l (k p) -> (l k) p", p=P), 4)
        vec("kv_norm", ins["kv_norm_2"], 2)
        vec("xa_q_gain", ins["xa_q_gain"].rearrange("l (k p) -> (l k) p", p=P), 4)
        vec("xa_k_gain", ins["xa_k_gain"].rearrange("l (k p) -> (l k) p", p=P), 4)
        vec("da_q_gain", ins["da_q_gain"], 1, 64, 2)
        vec("da_k_gain", ins["da_k_gain"], 1, 64, 2)
        for name in ("da_lam_q1", "da_lam_k1", "da_lam_q2", "da_lam_k2"):
            vec(name, ins[name], 1, 64)
        vec("da_sub_gain", ins["da_sub_gain"], 1)
        vec("b_f", ins["b_f_2"], 2, 6)
        vec("lam_re", ins["s5_lam_re"][0].rearrange("(k two) p -> k (two p)", two=2), 16)
        vec("lam_im", ins["s5_lam_im"][0].rearrange("(k two) p -> k (two p)", two=2), 16)
        at[0] = 2 * P
        for l in range(2):
            for j in range(3):
                vec(f"conv_w{l}{j}", rows_of(ins["conv_w_2"][l, j]), 44)
            vec(f"conv_b{l}", rows_of(ins["conv_b_2"][l]), 44)
        pieces = []
        for a, n, off, w, src in loads:
            r = 0
            while r < n:
                k = min(n - r, P - (a + r) % P)
                pieces.append((a + r, k, off, w, src[r:r + k]))
                r += k

        def colv(name, n=1, off=0):
            a = COLS[name] + off
            return col[:, a:a + n]

        def setup():
            tables = take(5, P)
            xrow, mrow = take(TT, D), take(TT, D)
            sq = take(TT, D)
            stat = take(8)
            consts_in, rows_in, vectors_in = sig("consts_in"), sig("rows_in"), sig("vectors_in")
            turned, moved, cleared = sig("turned"), sig("moved"), sig("cleared")

            @block.gpsimd
            def _(pool):
                pool.memset(tables, 0.0).then_inc(cleared.sem, cleared.tick())
                pool.memset(ones[:], 1.0).then_inc(cleared.sem, cleared.tick())
                for c, v in ((EPS_COL, EPS), (ZERO_COL, 0.0), (GN_COL, 1e-5 * 64), (RS_COL, 9 * LN2), (ONE_COL, 1.0)):
                    pool.memset(misc[:, c:c + 1], v).then_inc(cleared.sem, cleared.tick())

            @block.scalar
            def _(act):
                act.dma_start(ident[:], ins["c_ident"]).then_inc(consts_in.sem, consts_in.tick(16))
                act.dma_start(half_ones[:], ins["c_half_ones"]).then_inc(consts_in.sem, consts_in.tick(16))
                act.dma_start(xrow, ins["x"][0].rearrange("(t p) d -> p t d", p=P)).then_inc(rows_in.sem, rows_in.tick(16))
                act.dma_start(mrow, ins["mem"][0].rearrange("(t p) d -> p t d", p=P)).then_inc(rows_in.sem, rows_in.tick(16))
                act.wait_ge(cleared.sem, cleared.at(1))
                for a, n, off, w, src in pieces:
                    act.dma_start(tables[a % P:a % P + n, a // P, off:off + w], src)\
                       .then_inc(vectors_in.sem, vectors_in.tick(16))
                act.wait_ge(rows_in.sem, rows_in.at(32))
                act.wait_ge(cleared.sem, cleared.at(7))
                for t in range(TT):
                    act.activation(sq[:, t], mrow[:, t], ACT.Square, accum_out=stat[:, t:t + 1])\
                       .then_inc(act_own.sem, act_own.tick())
                act.wait_ge(act_own.sem, act_own.total)
                ordered(act, act_own, act.activation(stat[:, 2:4], stat[:, 0:2], ACT.Ln, scale=1.0 / D,
                                                     bias=misc[:, EPS_COL:EPS_COL + 1]))
                ordered(act, act_own, act.activation(stat[:, 4:6], stat[:, 2:4], ACT.Exp, scale=-0.5))
                for t in range(TT):
                    act.activation(mrow[:, t], mrow[:, t], ACT.Copy, scale=stat[:, 4 + t:5 + t])\
                       .then_inc(moved.sem, moved.tick())

            @block.tensor
            def _(pe):
                pe.wait_ge(consts_in.sem, consts_in.at(32))
                pe.wait_ge(vectors_in.sem, vectors_in.total)
                for n in range(5):
                    pe.transpose(bank[n][:, 0:P], tables[:, n], ident[:]).then_inc(turned.sem, turned.tick())
                pe.wait_ge(rows_in.sem, rows_in.at(32))
                pe.wait_ge(moved.sem, moved.at(2))
                for i, src in enumerate((xrow, mrow)):
                    for m in range(DT):
                        n = i * DT + m
                        b = bank[5 + n % 3]
                        if n >= 3:
                            pe.wait_ge(dve_own.sem, dve_own.at(5 + n - 2))
                        for t in range(TT):
                            mm = pe.transpose(b[:, t * P:(t + 1) * P], src[:, t, m * P:(m + 1) * P], ident[:])
                        mm.then_inc(turned.sem, turned.tick())

            @block.vector
            def _(dve):
                for n in range(5):
                    dve.wait_ge(turned.sem, turned.at(n + 1))
                    dve.tensor_copy(col[:, n * P:(n + 1) * P], bank[n][:, 0:P]).then_inc(dve_own.sem, dve_own.tick())
                for i, dst in enumerate((h, memn)):
                    for m in range(DT):
                        n = i * DT + m
                        dve.wait_ge(turned.sem, turned.at(6 + n))
                        dve.tensor_copy(dst[:, m], bank[5 + n % 3][:, 0:T]).then_inc(dve_own.sem, dve_own.tick())

            end_phase()
            release()

        def finish():
            rows = take(TT, D)
            turned, moved, stored = sig("turned"), sig("moved"), sig("stored")

            @block.tensor
            def _(pe):
                for n in range(DT * TT):
                    t, m = divmod(n, DT)
                    if n >= 4:
                        pe.wait_ge(moved.sem, moved.at(n - 3))
                    pe.transpose(bank[n % 4][:, 0:P], h[:, m, t * P:(t + 1) * P], ident[:])\
                      .then_inc(turned.sem, turned.tick())

            @block.vector
            def _(dve):
                for n in range(DT * TT):
                    t, m = divmod(n, DT)
                    dve.wait_ge(turned.sem, turned.at(n + 1))
                    dve.tensor_copy(rows[:, t, m * P:(m + 1) * P], bank[n % 4][:, 0:P])\
                       .then_inc(moved.sem, moved.tick())

            @block.scalar
            def _(act):
                for t in range(TT):
                    act.wait_ge(moved.sem, moved.at(DT * (t + 1)))
                    act.dma_start(out[0, t * P:(t + 1) * P, :], rows[:, t]).then_inc(stored.sem, stored.tick(16))
                act.wait_ge(stored.sem, stored.at(32))

        def norm(x, groups, div, gain, dst, summer=None, eps=EPS_COL, floor=None, work=None):
            mark = used[0]
            if work is not None:
                release(work)
            summer = ones[:] if summer is None else summer
            order = [t for g in groups for t in g]
            sq, lnv, rstd = take(len(order), T), take(2, T), take(2, T)
            squared, summed, rooted, normed = sig("squared"), sig("summed"), sig("rooted"), sig("normed")
            floored = sig("floored")

            @block.scalar
            def _(act):
                for n, t in enumerate(order):
                    act.activation(sq[:, n], x[:, t], ACT.Square).then_inc(squared.sem, squared.tick())
                done = 0
                for g, tiles in enumerate(groups):
                    act.wait_ge(summed.sem, summed.at(g + 1))
                    if g >= 2:
                        act.wait_ge(normed.sem, normed.at(done - len(groups[g - 1])))
                    src = bank[6 + g % 2][:, 0:T]
                    if floor is not None:
                        act.wait_ge(floored.sem, floored.at(g + 1))
                        src = rstd[:, g % 2]
                        ordered(act, act_own, act.activation(lnv[:, g % 2], src, ACT.Ln, scale=2.0 ** 18))
                        act.activation(rstd[:, g % 2], lnv[:, g % 2], ACT.Exp, scale=-0.5,
                                       bias=misc[:, RS_COL:RS_COL + 1]).then_inc(rooted.sem, rooted.tick())
                    else:
                        ordered(act, act_own, act.activation(lnv[:, g % 2], src, ACT.Ln, scale=1.0 / div,
                                                             bias=misc[:, eps:eps + 1]))
                        act.activation(rstd[:, g % 2], lnv[:, g % 2], ACT.Exp, scale=-0.5)\
                           .then_inc(rooted.sem, rooted.tick())
                    done += len(tiles)

            @block.tensor
            def _(pe):
                n = 0
                for g, tiles in enumerate(groups):
                    if g >= 2:
                        pe.wait_ge(rooted.sem, rooted.at(g - 1))
                    for i in range(len(tiles)):
                        pe.wait_ge(squared.sem, squared.at(n + 1))
                        mm = pe.matmul(bank[6 + g % 2][:, 0:T], summer, sq[:, n], start=i == 0, stop=i == len(tiles) - 1)
                        n += 1
                    mm.then_inc(summed.sem, summed.tick())

            @block.vector
            def _(dve):
                done = [0]
                for g, tiles in enumerate(groups):
                    if floor is not None:
                        dve.wait_ge(summed.sem, summed.at(g + 1))
                        if g >= 2:
                            dve.wait_ge(normed.sem, normed.at(g - 1))
                        dve.tensor_scalar(rstd[:, g % 2], bank[6 + g % 2][:, 0:T], floor, None, ALU.max)\
                           .then_inc(floored.sem, floored.tick())
                    dve.wait_ge(rooted.sem, rooted.at(g + 1))
                    for t in tiles:
                        dve.scalar_tensor_tensor(out=dst[:, t], in0=x[:, t], scalar=gain(t), in1=rstd[:, g % 2],
                                                 op0=ALU.mult, op1=ALU.mult).then_inc(normed.sem, normed.tick())

            end_phase()
            release(mark)

        def norm_model(x, name, layer, dst):
            norm(x, [list(range(DT))], D, lambda t: colv(name, 1, layer * DT + t), dst)

        def project(x, nk, tiles, evac, by="act", banks=None):
            banks = banks or bank[0:4]
            copied = sig("copied")
            marks = []

            @block.tensor
            def _(pe):
                marks.extend(stream(pe, tiles, x, nk, copied, banks))

            @(block.scalar if by == "act" else block.vector)
            def _(eng):
                for n, (_, _, m) in enumerate(tiles):
                    eng.wait_ge(tiles_done.sem, marks[n])
                    evac(eng, n, banks[n % len(banks)][0:m, 0:T]).then_inc(copied.sem, copied.tick())

            end_phase()

        def project_rows(x, nk, parts, dst, banks=None):
            banks = banks or bank[0:4]
            copied = sig("copied")
            marks = []

            @block.tensor
            def _(pe):
                n = 0
                for c, a, w, _ in parts:
                    need(pe, c)
                    for t in range(TT):
                        if n >= len(banks):
                            pe.wait_ge(copied.sem, copied.at(n - len(banks) + 1))
                        for k in range(nk):
                            mm = pe.matmul(banks[n % len(banks)][:, 0:w], x[:, k, t * P:(t + 1) * P],
                                           c.dst[:, k, a:a + w], start=k == 0, stop=k == nk - 1)
                        mm.then_inc(tiles_done.sem, tiles_done.tick())
                        marks.append(tiles_done.total)
                        n += 1
                    c.release = tiles_done.total

            @block.scalar
            def _(act):
                n = 0
                for c, a, w, to in parts:
                    for t in range(TT):
                        act.wait_ge(tiles_done.sem, marks[n])
                        act.activation(dst[:, t, to:to + w], banks[n % len(banks)][:, 0:w], ACT.Copy)\
                           .then_inc(copied.sem, copied.tick())
                        n += 1

            end_phase()

        def tiles_of(chunks, widths=None):
            return [(c, a, min(P, c.dst.shape[2] - a)) for c in chunks for a in range(0, c.dst.shape[2], P)]

        def add_to_h(eng, n, ps):
            return eng.tensor_tensor(h[:, n], ps, h[:, n], ALU.add)

        def attend(items):
            mark = used[0]
            C = len(items[0]["comps"])
            biased = items[0]["comps"][0][1] is not None
            s = take(2, C, T)
            p = take(2, C, T)
            pt = take(2, 2, P)
            small = take(2, 8)
            scored, soft_in, raised, weighed = sig("scored"), sig("soft_in"), sig("raised"), sig("weighed")
            turned, moved, mixed, stored = sig("turned"), sig("moved"), sig("mixed"), sig("out_copied")
            N = len(items)

            @block.tensor
            def _(pe):
                for i in range(N + 2):
                    if i < N:
                        it = items[i]
                        for c in range(C):
                            if i >= 2:
                                pe.wait_ge(raised.sem, raised.at(C * (i - 1)))
                            b = bank[(i % 2) * 2 + c]
                            prods = it["comps"][c][0]
                            for n, (l, r) in enumerate(prods):
                                mm = pe.matmul(b[:, 0:it["nk"]], l, r, start=n == 0, stop=n == len(prods) - 1)
                            mm.then_inc(scored.sem, scored.tick())
                    if 1 <= i <= N:
                        j = i - 1
                        pe.wait_ge(weighed.sem, weighed.at(j + 1))
                        if j >= 2:
                            pe.wait_ge(moved.sem, moved.at(j - 1))
                        for kt in range(items[j]["nk"] // P):
                            mm = pe.transpose(bank[4 + j % 2][:, kt * P:(kt + 1) * P],
                                              p[:, j % 2, 0, kt * P:(kt + 1) * P], ident[:])
                        mm.then_inc(turned.sem, turned.tick())
                    if i >= 2:
                        j = i - 2
                        it = items[j]
                        pe.wait_ge(moved.sem, moved.at(j + 1))
                        if j >= 2:
                            pe.wait_ge(stored.sem, stored.at(j - 1))
                        for m, (base, rows, val, _) in enumerate(it["outs"]):
                            for kt in range(it["nk"] // P):
                                mm = pe.matmul(bank[6 + j % 2][base:base + rows, m * P:(m + 1) * P], val(kt),
                                               pt[:, j % 2, kt], start=kt == 0, stop=kt == it["nk"] // P - 1)
                        mm.then_inc(mixed.sem, mixed.tick())

            @block.vector
            def _(dve):
                for i in range(N + 1):
                    if i < N:
                        it = items[i]
                        nk = it["nk"]
                        for c in range(C):
                            dve.wait_ge(scored.sem, scored.at(C * i + c + 1))
                            src = bank[(i % 2) * 2 + c][:, 0:nk]
                            sm = small[:, i % 2, 4 * c:4 * c + 4]
                            if biased:
                                if i >= 2:
                                    dve.wait_ge(raised.sem, raised.at(C * (i - 2) + c + 1))
                                ordered(dve, dve_own, dve.scalar_tensor_tensor(
                                    out=s[:, i % 2, c, 0:nk], in0=it["comps"][c][1], scalar=it["comps"][c][2], in1=src,
                                    op0=ALU.mult, op1=ALU.add))
                                src = s[:, i % 2, c, 0:nk]
                            ordered(dve, dve_own, dve.tensor_reduce(sm[:, 0:1], src, AX_X, ALU.max))
                            dve.tensor_scalar(sm[:, 1:2], sm[:, 0:1], -it["scale"], None, ALU.mult)\
                               .then_inc(soft_in.sem, soft_in.tick())
                    if i >= 1:
                        j = i - 1
                        nk = items[j]["nk"]
                        sm = small[:, j % 2]
                        dve.wait_ge(raised.sem, raised.at(C * (j + 1)))
                        for c in range(C):
                            ordered(dve, dve_own, dve.reciprocal(sm[:, 4 * c + 3:4 * c + 4], sm[:, 4 * c + 2:4 * c + 3]))
                        if C == 2:
                            ordered(dve, dve_own, dve.tensor_scalar(sm[:, 7:8], sm[:, 7:8], misc[:, NLAM:NLAM + 1],
                                                                    None, ALU.mult))
                            ordered(dve, dve_own, dve.tensor_scalar(p[:, j % 2, 0, 0:nk], p[:, j % 2, 0, 0:nk],
                                                                    sm[:, 3:4], None, ALU.mult))
                            dve.scalar_tensor_tensor(out=p[:, j % 2, 0, 0:nk], in0=p[:, j % 2, 1, 0:nk],
                                                     scalar=sm[:, 7:8], in1=p[:, j % 2, 0, 0:nk], op0=ALU.mult,
                                                     op1=ALU.add).then_inc(weighed.sem, weighed.tick())
                        else:
                            dve.tensor_scalar(p[:, j % 2, 0, 0:nk], p[:, j % 2, 0, 0:nk], sm[:, 3:4], None, ALU.mult)\
                               .then_inc(weighed.sem, weighed.tick())

            @block.scalar
            def _(act):
                for i in range(N + 2):
                    if i < N:
                        nk = items[i]["nk"]
                        for c in range(C):
                            act.wait_ge(soft_in.sem, soft_in.at(C * i + c + 1))
                            if i >= 2:
                                act.wait_ge(turned.sem, turned.at(i - 1))
                            src = s[:, i % 2, c, 0:nk] if biased else bank[(i % 2) * 2 + c][:, 0:nk]
                            sm = small[:, i % 2, 4 * c:4 * c + 4]
                            act.activation(p[:, i % 2, c, 0:nk], src, ACT.Exp, bias=sm[:, 1:2], scale=items[i]["scale"],
                                           accum_out=sm[:, 2:3]).then_inc(raised.sem, raised.tick())
                    if 1 <= i <= N:
                        j = i - 1
                        nk = items[j]["nk"]
                        act.wait_ge(turned.sem, turned.at(j + 1))
                        if j >= 2:
                            act.wait_ge(mixed.sem, mixed.at(j - 1))
                        act.activation(pt[:, j % 2, 0:nk // P], bank[4 + j % 2][:, 0:nk].rearrange("p (a b) -> p a b", b=P),
                                       ACT.Copy).then_inc(moved.sem, moved.tick())
                    if i >= 2:
                        j = i - 2
                        act.wait_ge(mixed.sem, mixed.at(j + 1))
                        for m, (base, rows, _, dst) in enumerate(items[j]["outs"]):
                            ins_ = act.activation(dst, bank[6 + j % 2][base:base + rows, m * P:(m + 1) * P], ACT.Copy)
                        ins_.then_inc(stored.sem, stored.tick())

            end_phase()
            release(mark)

        def cross_attention(l):
            mark = used[0]
            x = take(DT, T)
            q, k, v = take(DT, T), take(DT, T), take(TT, D)
            norm_model(h, "norm_xattn", l, x)
            cq = col_chunks(ins["xa_w_q"][l], range(0, D + 1, 256))
            project(x, DT, tiles_of(cq), lambda e, n, ps: e.activation(q[:, n], ps, ACT.Copy))
            heads = [[2 * i, 2 * i + 1] for i in range(4)]
            norm(q, heads, 256, lambda t: colv("xa_q_gain", 1, 2 * l + t % 2), q)

            @block.vector
            def _(dve):
                for t in range(DT):
                    dve.tensor_scalar(x[:, t], memn[:, t], colv("norm_mem", 1, l * DT + t), None, ALU.mult)

            end_phase()
            ck = col_chunks(ins["xa_w_kv"][l][:, 0:D], range(0, D + 1, 256))
            project(x, DT, tiles_of(ck), lambda e, n, ps: e.activation(k[:, n], ps, ACT.Copy))
            norm(k, heads, 256, lambda t: colv("xa_k_gain", 1, 2 * l + t % 2), k)
            cv = col_chunks(ins["xa_w_kv"][l][:, D:2 * D], range(0, D + 1, 256))
            project_rows(x, DT, [(c, 0, 256, 256 * i) for i, c in enumerate(cv)], v)
            o = x
            items = []
            for hd in range(4):
                for qt in range(TT):
                    qs = slice(qt * P, (qt + 1) * P)
                    items.append({
                        "nk": T, "scale": 256 ** -0.5,
                        "comps": [([(q[:, t, qs], k[:, t, :]) for t in heads[hd]], None, None)],
                        "outs": [(0, P, (lambda kt, m=2 * hd + m: v[:, kt, m * P:(m + 1) * P]), o[:, 2 * hd + m, qs])
                                 for m in range(2)]})
            attend(items)
            co = col_chunks(ins["xa_w_o"][l], range(0, D + 1, 256))
            project(o, DT, tiles_of(co), add_to_h, by="dve")
            release(mark)

        def down(acts, nf, chunks):
            @block.tensor
            def _(pe):
                per = chunks[0].dst.shape[1]
                for i, c in enumerate(chunks):
                    need(pe, c)
                    for kk in range(c.dst.shape[1]):
                        k = i * per + kk
                        for m in range(DT):
                            mm = pe.matmul(bank[4 + m // 2][:, (m % 2) * T:(m % 2 + 1) * T],
                                           c.dst[:, kk, m * P:(m + 1) * P], acts[:, k], start=k == 0 and m % 2 == 0,
                                           stop=k == nf - 1 and m % 2 == 1, skip_group_check=True)
                    mm.then_inc(tiles_done.sem, tiles_done.tick())
                    c.release = tiles_done.total
            return tiles_done.total

        def swiglu():
            mark = used[0]
            x, acts, sg = take(DT, T), take(FT, T), take(2, T)
            norm_model(h, "norm_ffn", 0, x)
            pairs = []
            for a in range(0, D_FF, 256):
                g = col_chunks(ins["ff_w_gate"][0][:, a:a + 256], (0, 256))[0]
                u = col_chunks(ins["ff_w_up"][0][:, a:a + 256], (0, 256))[0]
                pairs += [(g, u, 0), (g, u, P)]
            tiles = [(c, a, P) for g, u, a in pairs for c in (g, u)]
            gated, multiplied = sig("gated"), sig("multiplied")
            marks = []
            copied = sig("copied")

            @block.tensor
            def _(pe):
                marks.extend(stream(pe, tiles, x, DT, copied, bank[0:4]))

            @block.scalar
            def _(act):
                for i in range(FT):
                    act.wait_ge(tiles_done.sem, marks[2 * i])
                    if i >= 2:
                        act.wait_ge(copied.sem, copied.at(2 * (i - 1)))
                    act.activation(sg[:, i % 2], bank[2 * i % 4][:, 0:T], ACT.Silu).then_inc(gated.sem, gated.tick())

            @block.vector
            def _(dve):
                for i in range(FT):
                    dve.wait_ge(tiles_done.sem, marks[2 * i + 1])
                    dve.wait_ge(gated.sem, gated.at(i + 1))
                    dve.tensor_tensor(acts[:, i], bank[2 * i % 4 + 1][:, 0:T], sg[:, i % 2], ALU.mult)\
                       .then_inc(copied.sem, copied.tick(2))

            end_phase()
            done = down(acts, FT, row_chunks(ins["ff_w_down"][0]))
            add_down(tiles_done.total)
            end_phase()
            release(mark)

        def add_down(value, dst=None):
            dst = h if dst is None else dst

            @block.vector
            def _(dve):
                dve.wait_ge(tiles_done.sem, value)
                for b in range(4):
                    two = dst[:, 2 * b:2 * b + 2]
                    src = bank[4 + b][:, :].rearrange("p (a b) -> p a b", a=2)
                    if dst is h:
                        dve.tensor_tensor(two, src, two, ALU.add)
                    else:
                        dve.tensor_copy(two, src)

        def residual_norm(y, name, l):
            norm_model(y, name, l, y)

            @block.vector
            def _(dve):
                dve.tensor_tensor(h[:], h[:], y, ALU.add)

            end_phase()

        def load_const(dst, name, where=None):
            s_ = sig("consts_in")

            @block.scalar
            def _(act):
                act.dma_start(dst, ins[name]).then_inc(s_.sem, s_.tick(16))

        def diff_mixer():
            mark = used[0]
            x = take(DT, T)
            q, k, v = take(DT, T), take(DT, T), take(TT, D)
            kz = take(DT, 2, T)
            distance = take(T)
            lam = take(8)
            lam_ready, summed_lam, consts_in = sig("lam_ready"), sig("summed_lam"), sig("consts_in")
            load_const(distance, "c_distance")

            @block.gpsimd
            def _(pool):
                pool.memset(kz, 0.0)

            @block.vector
            def _(dve):
                for i, (a, b) in enumerate((("da_lam_q1", "da_lam_k1"), ("da_lam_q2", "da_lam_k2"))):
                    dve.tensor_tensor(lam[:, i:i + 1], colv(a), colv(b), ALU.mult)\
                       .then_inc(lam_ready.sem, lam_ready.tick())
                dve.tensor_scalar(misc[:, 8:9], colv("da_sub_gain"), 1.0 - LAMBDA_INIT, None, ALU.mult)

            @block.tensor
            def _(pe):
                pe.wait_ge(lam_ready.sem, lam_ready.at(2))
                pe.matmul(bank[5][:, 0:2], ones[:], lam[:, 0:2], start=True, stop=True)\
                  .then_inc(summed_lam.sem, summed_lam.tick())

            @block.scalar
            def _(act):
                act.wait_ge(summed_lam.sem, summed_lam.at(1))
                act.activation(lam[:, 2:4], bank[5][:, 0:2], ACT.Exp).then_inc(lam_ready.sem, lam_ready.tick())
                act.wait_ge(consts_in.sem, consts_in.at(16))

            @block.vector
            def _(dve):
                dve.wait_ge(lam_ready.sem, lam_ready.at(3))
                ordered(dve, dve_own, dve.tensor_tensor(lam[:, 4:5], lam[:, 3:4], lam[:, 2:3], ALU.subtract))
                dve.tensor_scalar(misc[:, NLAM:NLAM + 1], lam[:, 4:5], -LAMBDA_INIT, None, ALU.add)

            end_phase()
            norm_model(h, "norm_mix", 1, x)
            w = ins["da_w_qkv"][0]
            cqk = col_chunks(w[:, 0:2 * D], range(0, 2 * D + 1, 256))
            project(x, DT, tiles_of(cqk),
                    lambda e, n, ps: e.activation(q[:, n] if n < DT else k[:, n - DT], ps, ACT.Copy))
            cv = col_chunks(w[:, 2 * D:3 * D], range(0, D + 1, 256))
            project_rows(x, DT, [(c, 0, 256, 256 * i) for i, c in enumerate(cv)], v)
            single = [[t] for t in range(DT)]
            norm(q, single, 64, lambda t: colv("da_q_gain"), q, summer=half_ones[:])
            norm(k, single, 64, lambda t: colv("da_k_gain"), k, summer=half_ones[:])

            @block.vector
            def _(dve):
                for c in range(2):
                    r = slice(64 * c, 64 * c + 64)
                    dve.tensor_copy(kz[r, :, c, :], k[r])

            end_phase()
            o = x
            items = []
            for hd in range(DT):
                slope = 2.0 ** (-8.0 * (hd + 1) / DT)
                for qt in range(TT):
                    qs, nk = slice(qt * P, (qt + 1) * P), (qt + 1) * P
                    items.append({
                        "nk": nk, "scale": 0.125,
                        "comps": [([(q[:, hd, qs], kz[:, hd, c, 0:nk])], distance[:, T - nk:T], -slope * 8.0)
                                  for c in range(2)],
                        "outs": [(0, P, (lambda kt, m=hd: v[:, kt, m * P:(m + 1) * P]), o[:, hd, qs])]})
            attend(items)
            norm(o, single, P, lambda t: misc[:, 8:9], o)
            co = col_chunks(ins["da_w_o"][0], range(0, D + 1, 256))
            project(o, DT, tiles_of(co), add_to_h, by="dve")
            release(mark)

        t5 = {}

        def relative_bias():
            bias = t5["bias"] = take(6, T)
            mark = used[0]
            buckets, table, future = take(384), take(6), take(384)
            vec_, hank, flip = take(384), take(6, T), take(P)
            board = nc.dram_tensor("bias_board", (6, 384), F32, kind="Internal").ap()
            consts_in, product, ready = sig("consts_in"), sig("bias_product"), sig("bias_ready")
            boarded, flipped = sig("bias_boarded"), sig("bias_flipped")
            load_const(buckets[0:32], "c_buckets")
            load_const(table[0:32], "rel_bias_2")
            load_const(future[0:6], "c_future")
            load_const(flip, "c_flip")

            @block.tensor
            def _(pe):
                pe.wait_ge(consts_in.sem, consts_in.total)
                pe.matmul(bank[0][0:6, 0:384], table[0:32, :], buckets[0:32, :], start=True, stop=True)\
                  .then_inc(product.sem, product.tick())
                pe.wait_ge(boarded.sem, boarded.at(32))
                for n in range(6):
                    pe.matmul(bank[1 + n][:, 0:T], flip, hank[:, n], start=True, stop=True)\
                      .then_inc(flipped.sem, flipped.tick())

            @block.vector
            def _(dve):
                dve.wait_ge(consts_in.sem, consts_in.total)
                dve.wait_ge(product.sem, product.at(1))
                dve.tensor_tensor(vec_[0:6, :], bank[0][0:6, 0:384], future[0:6, :], ALU.add)\
                   .then_inc(ready.sem, ready.tick())
                for n in range(6):
                    dve.wait_ge(flipped.sem, flipped.at(n + 1))
                    dve.tensor_copy(bias[:, n], bank[1 + n][:, 0:T])

            @block.scalar
            def _(act):
                act.wait_ge(ready.sem, ready.at(1))
                act.dma_start(board, vec_[0:6, :]).then_inc(boarded.sem, boarded.tick(16))
                act.wait_ge(boarded.sem, boarded.at(16))
                diagonals = bass.AP(board.tensor, 0, [[1, P], [384, 6], [1, T]])
                act.dma_start(hank, diagonals).then_inc(boarded.sem, boarded.tick(16))

            end_phase()
            release(mark)

        def hybrid(l):
            if not t5:
                relative_bias()
            mark = used[0]
            x = take(DT, T)
            causal = take(T)
            aq, akz, av = take(3, T), take(6, T), take(TT, 384)
            fq, fkz, fv = take(3, T), take(6, T), take(TT, 384)
            cq, ckv = take(2, T), take(1, T)
            mq, mk, mv = take(5, T), take(4, T), take(TT, T)
            cos, sin, swap = take(T), take(T), take(96)
            sel, gate = take(6, T), take(6, T)
            rot = take(2, T)
            consts_in = sig("consts_in")
            load_const(causal, "c_causal")
            load_const(cos[0:96], "c_cos")
            load_const(sin[0:96], "c_sin")
            load_const(swap[0:96], "c_swap")

            @block.gpsimd
            def _(pool):
                pool.memset(akz, 0.0)
                pool.memset(fkz, 0.0)

            @block.vector
            def _(dve):
                dve.tensor_copy(sel[0:6], ident[0:6, 0:6, None].to_broadcast([6, 6, T]))

            @block.scalar
            def _(act):
                act.wait_ge(consts_in.sem, consts_in.total)

            norm_model(h, "ln_mix_pre_2", l, x)
            w = ins["w_in_2"][l]

            def padded(e, dst, n, ps):
                e.activation(dst[0:64, 2 * n], ps[0:64], ACT.Copy)
                return e.activation(dst[64:P, 2 * n + 1], ps[64:P], ACT.Copy)

            tiles = tiles_of(col_chunks(w, range(0, 769, 256)))
            tiles += tiles_of(col_chunks(w, (1152, 1408)))
            c = col_chunks(w, (1408, 1568))[0]
            tiles += [(c, 0, P), (c, 64, 96)]
            tiles += tiles_of(col_chunks(w, range(1568, 2337, 256)))

            def evac(e, n, ps):
                if n < 3:
                    return e.activation(aq[:, n], ps, ACT.Copy)
                if n < 6:
                    return padded(e, akz, n - 3, ps)
                if n < 8:
                    return e.activation(cq[:, n - 6], ps, ACT.Copy)
                if n == 8:
                    return e.activation(ckv[:, 0], ps, ACT.Copy)
                if n == 9:
                    return e.activation(mq[0:96, 4], ps, ACT.Copy)
                if n < 13:
                    return e.activation(fq[:, n - 10], ps, ACT.Copy)
                return padded(e, fkz, n - 13, ps)

            project(x, DT, tiles, evac)
            ca = col_chunks(w, (768, 1024, 1152))
            cf = col_chunks(w, (2336, 2592, 2726))
            project_rows(x, DT, [(ca[0], 0, 256, 0), (ca[1], 0, P, 256)], av)
            project_rows(x, DT, [(cf[0], 0, 256, 0), (cf[1], 0, P, 256)], fv)
            z, az, lz, dec, dq, nd = (gate[:, i] for i in range(6))
            product, ready = sig("gate_product"), sig("gate_ready")

            @block.tensor
            def _(pe):
                for k in range(DT):
                    mm = pe.matmul(bank[0][0:6, 0:T], cf[1].dst[:, k, P:P + 6], x[:, k], start=k == 0, stop=k == DT - 1)
                mm.then_inc(tiles_done.sem, tiles_done.tick())
                cf[1].release = tiles_done.total

            got = tiles_done.total
            r6 = slice(0, 6)

            @block.vector
            def _(dve):
                dve.wait_ge(tiles_done.sem, got)
                ordered(dve, dve_own, dve.tensor_scalar(z[r6], bank[0][r6, 0:T], colv("b_f", 1, l)[r6], None, ALU.add))
                dve.scalar_tensor_tensor(out=az[r6], in0=z[r6], scalar=-1.0, in1=z[r6], op0=ALU.mult, op1=ALU.max)\
                   .then_inc(ready.sem, ready.tick())

            @block.scalar
            def _(act):
                act.wait_ge(ready.sem, ready.at(1))
                ordered(act, act_own, act.activation(lz[r6], az[r6], ACT.Exp, scale=-1.0))
                act.activation(az[r6], lz[r6], ACT.Ln, bias=misc[r6, ONE_COL:ONE_COL + 1])\
                   .then_inc(ready.sem, ready.tick())

            @block.vector
            def _(dve):
                dve.wait_ge(ready.sem, ready.at(2))
                ordered(dve, dve_own, dve.scalar_tensor_tensor(out=lz[r6], in0=z[r6], scalar=0.0, in1=az[r6],
                                                               op0=ALU.min, op1=ALU.subtract))
                ordered(dve, dve_own, dve.tensor_tensor_scan(dec[r6], ones[r6, 0:1].to_broadcast([6, T]), lz[r6], 0.0,
                                                             ALU.mult, ALU.add))
                dve.tensor_scalar(dq[r6], dec[r6], 8.0, None, ALU.mult)
                dve.tensor_scalar(nd[r6], dec[r6], -8.0, None, ALU.mult)

            end_phase()
            norm(cq, [[0, 1]], 256, lambda t: colv("q_norm", 1, 2 * l + t), cq)
            norm(ckv, [[0]], P, lambda t: colv("kv_norm", 1, l), ckv)
            uq = col_chunks(ins["w_uq_2"][l], (0, 384))[0]
            project(cq, 2, [(uq, 96 * i, 96) for i in range(4)],
                    lambda e, n, ps: e.activation(mq[0:96, n], ps, ACT.Copy))
            ukv = col_chunks(ins["w_ukv_2"][l], (0, 512))[0]
            project(ckv, 1, [(ukv, P * i, 64) for i in range(4)],
                    lambda e, n, ps: e.activation(mk[0:64, n], ps, ACT.Copy))
            turned, rotated = sig("turned"), sig("rotated")

            @block.tensor
            def _(pe):
                for t in range(TT):
                    mm = pe.matmul(bank[t][:, 0:T].rearrange("p (a b) -> p a b", a=4), ckv[:, 0, t * P:(t + 1) * P],
                                   ukv.dst[:, 0].rearrange("p (a two b) -> p a two b", a=4, two=2)[:, :, 1, :],
                                   start=True, stop=True)
                mm.then_inc(tiles_done.sem, tiles_done.tick())
                ukv.release = tiles_done.total
                for i in range(5):
                    if i >= 2:
                        pe.wait_ge(rotated.sem, rotated.at(i - 1))
                    pe.matmul(bank[2 + i % 2][0:96, 0:T], swap[0:96], mq[0:96, i], start=True, stop=True)\
                      .then_inc(turned.sem, turned.tick())

            got2 = tiles_done.total

            @block.scalar
            def _(act):
                act.wait_ge(tiles_done.sem, got2)
                for t in range(TT):
                    act.activation(mv[:, t], bank[t][:, 0:T], ACT.Copy)

            @block.vector
            def _(dve):
                for i in range(5):
                    dve.wait_ge(turned.sem, turned.at(i + 1))
                    ordered(dve, dve_own, dve.tensor_tensor(rot[0:96, 0], bank[2 + i % 2][0:96, 0:T], sin[0:96], ALU.mult))
                    ordered(dve, dve_own, dve.tensor_tensor(rot[0:96, 1], mq[0:96, i], cos[0:96], ALU.mult))
                    dve.tensor_tensor(mq[0:96, i], rot[0:96, 1], rot[0:96, 0], ALU.add)\
                       .then_inc(rotated.sem, rotated.tick())
                    dve.wait_ge(rotated.sem, rotated.at(i + 1))
                dve.tensor_copy(mk[64:96], mq[64:96, 4:5].to_broadcast([32, 4, T]))

            end_phase()
            o = x
            bias = t5["bias"]
            items = []
            for hd in range(16):
                for qt in range(TT):
                    qs, nk = slice(qt * P, (qt + 1) * P), (qt + 1) * P
                    if hd < 6:
                        i = hd
                        prods = [(aq[:, i // 2, qs], akz[:, i, 0:nk])]
                        comp, scale, val = (prods, bias[:, i, T - nk:T], 8.0), 0.125, (av, 64 * i)
                    elif hd < 10:
                        i = hd - 6
                        prods = [(mq[0:96, i, qs], mk[0:96, i, 0:nk])]
                        comp, scale, val = (prods, causal[:, T - nk:T], 1.0), 96 ** -0.5, (mv, 64 * i)
                    else:
                        i = hd - 10
                        prods = [(fq[:, i // 2, qs], fkz[:, i, 0:nk]), (sel[r6, i, 0:P], nd[r6, 0:nk]),
                                 (dq[r6, qs], sel[r6, i, 0:nk])]
                        comp, scale, val = (prods, causal[:, T - nk:T], 1.0), 0.125, (fv, 64 * i)
                    base = 64 * (hd % 2)
                    items.append({"nk": nk, "scale": scale, "comps": [comp], "outs": [
                        (base, 64, (lambda kt, v=val: v[0][:, kt, v[1]:v[1] + 64]), o[base:base + 64, hd // 2, qs])]})
            attend(items)
            y = take(DT, T)
            co = col_chunks(ins["w_o_2"][l], range(0, D + 1, 256))
            project(o, DT, tiles_of(co), lambda e, n, ps: e.activation(y[:, n], ps, ACT.Copy))
            residual_norm(y, "ln_mix_post_2", l)
            release(mark)

        def conv_ffn(l):
            mark = used[0]
            x, acts, y = take(DT, T), take(FT, T), take(DT, T)
            u, gl = take(4, T), take(2, T)
            norm_model(h, "ln_ffn_pre_2", l, x)
            w = ins["w_up_2"][l]
            tiles = []
            for a in range(0, D_FF, 256):
                g, v = col_chunks(w, (a, a + 256))[0], col_chunks(w, (D_FF + a, D_FF + a + 256))[0]
                tiles += [(g, 0, P), (v, 0, P), (g, P, P), (v, P, P)]
            copied, based, convolved, gelu, multiplied = (sig(n) for n in ("copied", "based", "convolved", "gelu", "multiplied"))
            marks = []

            def taps(j, n):
                return colv(f"conv_{j}", 1, n // 2 + FT * (n % 2))

            @block.tensor
            def _(pe):
                marks.extend(stream(pe, tiles, x, DT, convolved, bank[0:4]))

            @block.scalar
            def _(act):
                for n in range(2 * FT + 2):
                    if n < 2 * FT:
                        act.wait_ge(tiles_done.sem, marks[n])
                        if n >= 4 and n % 2:
                            act.wait_ge(multiplied.sem, multiplied.at(n // 2 - 1))
                        elif n >= 4:
                            act.wait_ge(gelu.sem, gelu.at(n // 2 - 1))
                        act.activation(u[:, n % 4], bank[n % 4][:, 0:T], ACT.Identity, scale=taps(f"w{l}2", n),
                                       bias=taps(f"b{l}", n)).then_inc(based.sem, based.tick())
                    if n >= 2 and n % 2 == 0:
                        i = n // 2 - 1
                        act.wait_ge(convolved.sem, convolved.at(2 * i + 1))
                        if i >= 2:
                            act.wait_ge(multiplied.sem, multiplied.at(i - 1))
                        act.activation(gl[:, i % 2], u[:, 2 * i % 4], ACT.Gelu_apprx_tanh).then_inc(gelu.sem, gelu.tick())

            @block.vector
            def _(dve):
                for n in range(2 * FT + 2):
                    if n < 2 * FT:
                        ps = bank[n % 4]
                        dve.wait_ge(based.sem, based.at(n + 1))
                        ordered(dve, dve_own, dve.scalar_tensor_tensor(
                            out=u[:, n % 4, 1:T], in0=ps[:, 0:T - 1], scalar=taps(f"w{l}1", n), in1=u[:, n % 4, 1:T],
                            op0=ALU.mult, op1=ALU.add))
                        ins_ = dve.scalar_tensor_tensor(
                            out=u[:, n % 4, 2:T], in0=ps[:, 0:T - 2], scalar=taps(f"w{l}0", n), in1=u[:, n % 4, 2:T],
                            op0=ALU.mult, op1=ALU.add)
                        ins_.then_inc(convolved.sem, convolved.tick())
                    if n >= 3 and n % 2:
                        i = (n - 3) // 2
                        dve.wait_ge(gelu.sem, gelu.at(i + 1))
                        dve.wait_ge(convolved.sem, convolved.at(2 * i + 2))
                        dve.tensor_tensor(acts[:, i], gl[:, i % 2], u[:, (2 * i + 1) % 4], ALU.mult)\
                           .then_inc(multiplied.sem, multiplied.tick())

            end_phase()
            down(acts, FT, row_chunks(ins["w_down_2"][l]))
            add_down(tiles_done.total, y)
            end_phase()
            residual_norm(y, "ln_ffn_post_2", l)
            release(mark)

        def layer0_mixer():
            mark = used[0]
            y = take(DT, T)
            hn = scratch[:, SCRATCH - DT * T:].rearrange("p (a b) -> p a b", a=DT)
            norm_model(h, "norm_mix", 0, hn)
            s5(hn, y[:, 4:8])
            rwkv(hn, y[:, 0:4])
            co = col_chunks(ins["hy_w_out"][0], range(0, D + 1, 256))
            project(y, DT, tiles_of(co), add_to_h, by="dve")
            release(mark)

        def s5(hn, yb):
            G, S = 32, 16
            mark = used[0]
            u = take(4, T)
            c0 = RW * 3 + 288
            project(hn, DT, tiles_of(col_chunks(ins["hy_w_in"][0], (c0, c0 + 256, c0 + 512))),
                    lambda e, n, ps: e.activation(u[:, n], ps, ACT.Copy))
            cosw, sinw = take(S, T), take(S, T)
            bt, ct = take(2, S, P), take(2, S, P)
            work = used[0]
            par = take(12, S)
            bn, bb, bw = take(2, S, 16), take(2, S, 16), take(2, S, 16)
            cn = take(2, 4, P)
            wide = take(S, P)
            ta, tb = take(S, P), take(S, P)
            ldt = take(G)
            dt, th, mag, k1, s_h, num_r, num_i, den, c_r, c_i, t0 = (par[:, i] for i in range(11))
            lre, lim = colv("lam_re", S), colv("lam_im", S)
            loaded, zeroed, ready = sig("s5_loaded"), sig("s5_zeroed"), sig("s5_ready")

            @block.scalar
            def _(act):
                step = ins["s5_log_dt"].to_broadcast([64, G])
                for a in range(2):
                    act.dma_start(ldt[64 * a:64 * a + 64], step)\
                       .then_inc(loaded.sem, loaded.tick(16))
                for i, n in enumerate(("s5_b_re", "s5_b_im")):
                    act.dma_start(bn[:, i], ins[n][0].rearrange("(j two) p i -> (two p) j i", two=2))\
                       .then_inc(loaded.sem, loaded.tick(16))
                for i, n in enumerate(("s5_c_re", "s5_c_im")):
                    rows = ins[n][0].rearrange("g i p -> (g i) p").rearrange("(m q) p -> q m p", q=P)
                    for a in range(2):
                        act.dma_start(cn[:, i, :, 64 * a:64 * a + 64], rows).then_inc(loaded.sem, loaded.tick(16))
                act.wait_ge(loaded.sem, loaded.at(16 * 8))
                act.activation(dt[0:64], ldt[0:64, 0:G:2], ACT.Exp)
                act.activation(dt[64:P], ldt[64:P, 1:G:2], ACT.Exp).then_inc(ready.sem, ready.tick())

            @block.gpsimd
            def _(pool):
                pool.memset(wide, 0.0).then_inc(zeroed.sem, zeroed.tick())
                pool.memset(ct, 0.0).then_inc(zeroed.sem, zeroed.tick())

            @block.vector
            def _(dve):
                def o(i_):
                    ordered(dve, dve_own, i_)
                dve.wait_ge(ready.sem, ready.at(1))
                o(dve.tensor_tensor(th, lim, dt, ALU.mult))
                o(dve.tensor_tensor(t0, lre, dt, ALU.mult))
                o(dve.tensor_scalar(k1, th, float(1 / (2 * np.pi)), None, ALU.mult))
                o(dve.tensor_scalar(k1, k1, 12582912.0, None, ALU.add))
                o(dve.tensor_scalar(k1, k1, -12582912.0, None, ALU.add))
                for part in (6.28125, 0.0019340515136718750, float(2 * np.pi - 6.28125 - 0.0019340515136718750)):
                    o(dve.scalar_tensor_tensor(out=th, in0=k1, scalar=-part, in1=th, op0=ALU.mult, op1=ALU.add))
                o(dve.tensor_scalar(th, th, 3.1415925, -3.1415925, ALU.min, ALU.max))
                dve.tensor_scalar(s_h, th, 0.5, None, ALU.mult).then_inc(ready.sem, ready.tick())

            @block.scalar
            def _(act):
                act.wait_ge(ready.sem, ready.at(2))
                act.activation(mag, t0, ACT.Exp).then_inc(act_own.sem, act_own.tick())
                act.activation(sinw[:, :, 0], th, ACT.Sin).then_inc(act_own.sem, act_own.tick())
                act.activation(k1, s_h, ACT.Sin).then_inc(ready.sem, ready.tick())

            @block.vector
            def _(dve):
                def o(i_):
                    ordered(dve, dve_own, i_)
                dve.wait_ge(ready.sem, ready.at(3))
                o(dve.scalar_tensor_tensor(out=den, in0=k1, scalar=-2.0, in1=k1, op0=ALU.mult, op1=ALU.mult))
                o(dve.tensor_scalar(cosw[:, :, 0], den, 1.0, None, ALU.add))
                o(dve.tensor_tensor(num_r, mag, cosw[:, :, 0], ALU.mult))
                o(dve.tensor_scalar(num_r, num_r, -1.0, None, ALU.add))
                o(dve.tensor_tensor(num_i, mag, sinw[:, :, 0], ALU.mult))
                o(dve.tensor_tensor(den, lre, lre, ALU.mult))
                o(dve.tensor_tensor(k1, lim, lim, ALU.mult))
                o(dve.tensor_tensor(den, den, k1, ALU.add))
                o(dve.reciprocal(k1, den))
                o(dve.tensor_tensor(c_r, num_r, lre, ALU.mult))
                o(dve.tensor_tensor(t0, num_i, lim, ALU.mult))
                o(dve.tensor_tensor(c_r, c_r, t0, ALU.add))
                o(dve.tensor_tensor(c_r, c_r, k1, ALU.mult))
                o(dve.tensor_tensor(c_i, num_i, lre, ALU.mult))
                o(dve.tensor_tensor(t0, num_r, lim, ALU.mult))
                o(dve.tensor_tensor(c_i, c_i, t0, ALU.subtract))
                o(dve.tensor_tensor(c_i, c_i, k1, ALU.mult))
                cr, ci = (v[:, :, None].to_broadcast([P, S, 16]) for v in (c_r, c_i))
                for dst, (x1, x2, op) in enumerate(((0, 1, ALU.subtract), (1, 0, ALU.add))):
                    o(dve.tensor_tensor(bw[:, 0], bn[:, x1], cr, ALU.mult))
                    o(dve.tensor_tensor(bw[:, 1], bn[:, x2], ci, ALU.mult))
                    o(dve.tensor_tensor(bb[:, dst], bw[:, 0], bw[:, 1], op))
                dve.wait_ge(zeroed.sem, zeroed.at(2))
                spread, turned, filled = sig("s5_spread"), sig("turned"), sig("s5_filled")
                for i in range(2):
                    if i:
                        dve.wait_ge(turned.sem, turned.at(4))
                    for a in range(2):
                        for q in range(4):
                            ins_ = dve.tensor_copy(wide[64 * a:64 * a + 64, q:S:4, (2 * q + a) * 16:(2 * q + a + 1) * 16],
                                                   bb[64 * a:64 * a + 64, i, q:S:4, :])
                    ins_.then_inc(spread.sem, spread.tick())
                m = 1
                while m < T:
                    cm, sm = (v[:, :, m - 1:m].to_broadcast([P, S, m]) for v in (cosw, sinw))
                    a_, b_ = ta[:, :, 0:m], tb[:, :, 0:m]
                    c1, s1 = cosw[:, :, 0:m], sinw[:, :, 0:m]
                    o(dve.tensor_tensor(a_, c1, cm, ALU.mult))
                    o(dve.tensor_tensor(b_, s1, sm, ALU.mult))
                    o(dve.tensor_tensor(cosw[:, :, m:2 * m], a_, b_, ALU.subtract))
                    o(dve.tensor_tensor(a_, s1, cm, ALU.mult))
                    o(dve.tensor_tensor(b_, c1, sm, ALU.mult))
                    o(dve.tensor_tensor(sinw[:, :, m:2 * m], a_, b_, ALU.add))
                    m *= 2

            spread, turned, filled = sig("s5_spread"), sig("turned"), sig("s5_filled")

            @block.tensor
            def _(pe):
                for i in range(2):
                    pe.wait_ge(spread.sem, spread.at(i + 1))
                    for b in range(4):
                        if i:
                            pe.wait_ge(filled.sem, filled.at(b + 1))
                        for q in range(4):
                            mm = pe.transpose(bank[b][:, q * P:(q + 1) * P], wide[:, 4 * b + q], ident[:])
                        mm.then_inc(turned.sem, turned.tick())
                pe.wait_ge(loaded.sem, loaded.at(16 * 8))
                for i in range(2):
                    for m in range(4):
                        mm = pe.transpose(bank[4 + i][:, m * P:(m + 1) * P], cn[:, i, m], ident[:])
                    mm.then_inc(turned.sem, turned.tick())

            @block.scalar
            def _(act):
                for i in range(2):
                    for b in range(4):
                        act.wait_ge(turned.sem, turned.at(4 * i + b + 1))
                        act.activation(bt[:, i, 4 * b:4 * b + 4], bank[b][:, :].rearrange("p (a b) -> p a b", a=4), ACT.Copy)\
                           .then_inc(filled.sem, filled.tick())
                act.wait_ge(zeroed.sem, zeroed.at(2))
                for i in range(2):
                    act.wait_ge(turned.sem, turned.at(9 + i))
                    src = bank[4 + i][:, :].rearrange("p (a b) -> p a b", a=4)
                    for a in range(2):
                        for q in range(4):
                            cols = slice((2 * q + a) * 16, (2 * q + a + 1) * 16)
                            act.activation(ct[64 * a:64 * a + 64, i, q:S:4, cols], src[64 * a:64 * a + 64, :, cols],
                                           ACT.Copy, scale=1.0 if i == 0 else -1.0)

            end_phase()
            release(work)
            par = take(12, S)
            mags = mag
            mod, pa, pb = take(2, 2, T), take(2, 2, T), take(2, 2, T)
            z = take(2, 2, T)

            drive, scanned, state, used_state = sig("s5_drive"), sig("s5_scanned"), sig("s5_state"), sig("s5_output")
            modulated = sig("s5_modulated")

            @block.tensor
            def _(pe):
                for j in range(S + 1):
                    if j < S:
                        if j >= 2:
                            pe.wait_ge(modulated.sem, modulated.at(j - 1))
                        for i in range(2):
                            mm = pe.matmul(bank[j % 2][:, i * T:(i + 1) * T], bt[:, i, j], u[:, j // 4], start=True, stop=True)
                        mm.then_inc(drive.sem, drive.tick())
                    if j >= 1:
                        k = j - 1
                        pe.wait_ge(state.sem, state.at(k + 1))
                        for i in range(2):
                            mm = pe.matmul(bank[4 + k // 4][:, 0:T], ct[:, i, k], pa[:, k % 2, i],
                                           start=k % 4 == 0 and i == 0, stop=k % 4 == 3 and i == 1)
                        mm.then_inc(used_state.sem, used_state.tick())

            @block.vector
            def _(dve):
                def o(i_):
                    ordered(dve, dve_own, i_)
                for j in range(S):
                    b = j % 2
                    src = bank[b][:, :].rearrange("p (a b) -> p a b", a=2)
                    cc, ss = (v[:, j:j + 1].to_broadcast([P, 2, T]) for v in (cosw, sinw))
                    dve.wait_ge(drive.sem, drive.at(j + 1))
                    if j >= 2:
                        dve.wait_ge(used_state.sem, used_state.at(j - 1))
                    dve.tensor_tensor(pa[:, b], src, cc, ALU.mult)
                    dve.tensor_tensor(pb[:, b], src, ss, ALU.mult).then_inc(modulated.sem, modulated.tick())
                    dve.wait_ge(modulated.sem, modulated.at(j + 1))
                    dve.tensor_tensor(mod[:, b, 0], pa[:, b, 0], pb[:, b, 1], ALU.add).then_inc(dve_own.sem, dve_own.tick())
                    o(dve.tensor_tensor(mod[:, b, 1], pa[:, b, 1], pb[:, b, 0], ALU.subtract))
                    dve.tensor_tensor_scan(z[:, b, 0], mags[:, j:j + 1].to_broadcast([P, T]), mod[:, b, 0], 0.0,
                                           ALU.mult, ALU.add).then_inc(dve_own.sem, dve_own.tick())
                    o(dve.tensor_tensor_scan(z[:, b, 1], mags[:, j:j + 1].to_broadcast([P, T]), mod[:, b, 1], 0.0,
                                             ALU.mult, ALU.add))
                    dve.tensor_tensor(mod[:, b], z[:, b], cc, ALU.mult).then_inc(dve_own.sem, dve_own.tick())
                    o(dve.tensor_tensor(pb[:, b], z[:, b], ss, ALU.mult))
                    dve.tensor_tensor(pa[:, b, 0], mod[:, b, 0], pb[:, b, 1], ALU.subtract)\
                       .then_inc(dve_own.sem, dve_own.tick())
                    dve.tensor_tensor(pa[:, b, 1], mod[:, b, 1], pb[:, b, 0], ALU.add).then_inc(state.sem, state.tick())
                    dve.wait_ge(state.sem, state.at(j + 1))
                dve.wait_ge(used_state.sem, used_state.at(S))
                for m in range(4):
                    dve.scalar_tensor_tensor(out=u[:, m], in0=u[:, m], scalar=colv("s5_d", 1, m),
                                             in1=bank[4 + m][:, 0:T], op0=ALU.mult, op1=ALU.add)

            end_phase()
            sg = take(4, T)

            @block.scalar
            def _(act):
                act.activation(u, u, ACT.Gelu_apprx_tanh)

            end_phase()
            glu = col_chunks(ins["s5_w_glu"][0], (0, 512))
            project(u, 4, tiles_of(glu),
                    lambda e, n, ps: e.activation(sg[:, n], ps, ACT.Sigmoid, bias=colv("s5_b_glu", 1, n)))

            @block.vector
            def _(dve):
                dve.tensor_tensor(yb, u, sg, ALU.mult)

            end_phase()
            release(mark)

        def rwkv(hn, ya):
            mark = used[0]
            bonus, g, v = take(4, T), take(4, T), take(4, T)
            kr = take(4, NCH, 2, 64)
            turns = used[0]
            vt, kct, bct = (take(NCH, RW) for _ in range(3))
            last = take(4, NCH)
            pads = used[0]
            kz, bz = take(8, T), take(8, T)
            zone = used[0]
            r, k, lo = take(4, T), take(4, T), take(4, T)
            lw = take(4, RW)
            ld, cum, a, kk = take(4, T), take(4, T), take(4, T), take(4, T)
            el, ei, bf, kf = (take(4, T) for _ in range(4))
            tmp = kct.rearrange("p a b -> p (a b)")[:, 0:4 * T].rearrange("p (a b) -> p a b", a=4)
            om = take(20)
            assert used[0] <= SCRATCH - DT * T
            dsts = [(v_, j) for v_ in (r, k, v) for j in range(4)] + [(lo, j) for j in range(4)]
            w = ins["hy_w_in"][0]
            tiles = tiles_of(col_chunks(w, range(0, 3 * RW + 1, 256)))
            c = col_chunks(w, (1536, 1664, 1824))
            tiles += [(c[0], 0, 64), (c[0], 64, 64), (c[1], 0, P), (c[1], P, 32)]
            based, shifted, loaded = sig("based"), sig("shifted"), sig("lora_loaded")
            marks = []

            @block.vector
            def _(dve):
                dve.tensor_scalar(om[:, 0:16], colv("mu", 16), -1.0, 1.0, ALU.mult, ALU.add)\
                   .then_inc(shifted.sem, shifted.tick())
                dve.tensor_scalar(om[:, 16:20], colv("rw_k_a", 4), -1.0, 1.0, ALU.mult, ALU.add)

            @block.gpsimd
            def _(pool):
                pool.memset(kz, 0.0)
                pool.memset(bz, 0.0)

            @block.tensor
            def _(pe):
                marks.extend(stream(pe, tiles, hn, DT, shifted, bank[0:4], 1))

            @block.scalar
            def _(act):
                for i, (n, a0, a1) in enumerate((("rw_w_up", 0, 64), ("rw_a_up", 0, 64), ("rw_g_up", 0, P),
                                                 ("rw_g_up", P, 160))):
                    act.dma_start(lw[0:a1 - a0, i], ins[n][0, a0:a1]).then_inc(loaded.sem, loaded.tick(16))
                act.wait_ge(shifted.sem, shifted.at(1))
                for n, (d, j) in enumerate(dsts):
                    m = tiles[n][2]
                    act.wait_ge(tiles_done.sem, marks[n])
                    act.activation(d[0:m, j], bank[n % 4][0:m, 0:T], ACT.Copy, scale=om[0:m, n:n + 1])\
                       .then_inc(based.sem, based.tick())
                act.wait_ge(loaded.sem, loaded.at(64))

            @block.vector
            def _(dve):
                for n, (d, j) in enumerate(dsts):
                    m = tiles[n][2]
                    dve.wait_ge(based.sem, based.at(n + 1))
                    dve.scalar_tensor_tensor(out=d[0:m, j, 1:T], in0=bank[n % 4][0:m, 0:T - 1],
                                             scalar=colv("mu", 1, n)[0:m], in1=d[0:m, j, 1:T], op0=ALU.mult,
                                             op1=ALU.add).then_inc(shifted.sem, shifted.tick())

            end_phase()

            @block.scalar
            def _(act):
                act.activation(lo[0:64, 0], lo[0:64, 0], ACT.Tanh)
                act.activation(lo[:, 2], lo[:, 2], ACT.Sigmoid)
                act.activation(lo[0:32, 3], lo[0:32, 3], ACT.Sigmoid)

            end_phase()
            raised, taken = sig("lora_product"), sig("lora_taken")

            @block.tensor
            def _(pe):
                n = 0
                for part in range(3):
                    for j in range(4):
                        if n >= 4:
                            pe.wait_ge(taken.sem, taken.at(n - 3))
                        b = bank[n % 4][:, 0:T]
                        cs = slice(j * P, (j + 1) * P)
                        if part < 2:
                            mm = pe.matmul(b, lw[0:64, part, cs], lo[0:64, part], start=True, stop=True)
                        else:
                            pe.matmul(b, lw[:, 2, cs], lo[:, 2], start=True, stop=False)
                            mm = pe.matmul(b, lw[0:32, 3, cs], lo[0:32, 3], start=False, stop=True)
                        mm.then_inc(raised.sem, raised.tick())
                        n += 1

            @block.scalar
            def _(act):
                for n in range(12):
                    part, j = divmod(n, 4)
                    act.wait_ge(raised.sem, raised.at(n + 1))
                    src = bank[n % 4][:, 0:T]
                    if part < 2:
                        i_ = act.activation((ld, a)[part][:, j], src, ACT.Sigmoid, bias=colv(("rw_w0", "rw_a0")[part], 1, j))
                    else:
                        i_ = act.activation(g[:, j], src, ACT.Copy)
                    i_.then_inc(taken.sem, taken.tick())

            @block.vector
            def _(dve):
                for j in range(4):
                    dve.tensor_scalar(kk[:, j], k[:, j], colv("rw_k_k", 1, j), None, ALU.mult)

            end_phase()
            norm(kk, [[j] for j in range(4)], 1, lambda t: misc[:, ONE_COL:ONE_COL + 1], kk, summer=half_ones[:],
                 floor=1e-24, work=turns)
            ready, summed, copied = sig("rw_ready"), sig("rw_summed"), sig("copied")
            turned = sig("turned")

            @block.vector
            def _(dve):
                def o(i_):
                    ordered(dve, dve_own, i_)
                o(dve.tensor_scalar(ld, ld, -float(np.exp(-0.5)), None, ALU.mult))
                for j in range(4):
                    for cc in range(NCH):
                        s = slice(cc * 64, cc * 64 + 64)
                        dve.tensor_tensor_scan(cum[:, j, s], ones[:, 0:64], ld[:, j, s], 0.0, ALU.mult, ALU.add)\
                           .then_inc(dve_own.sem, dve_own.tick())
                dve.wait_ge(dve_own.sem, dve_own.total)
                dve.tensor_tensor(tmp, cum, ld, ALU.subtract).then_inc(ready.sem, ready.tick())
                o(dve.tensor_tensor(bf, kk, a, ALU.mult))
                for j in range(4):
                    o(dve.tensor_scalar(a[:, j], a[:, j], colv("rw_k_a", 1, j), om[:, 16 + j:17 + j], ALU.mult, ALU.add))
                o(dve.tensor_tensor(k, k, a, ALU.mult))
                o(dve.tensor_tensor(a, r, k, ALU.mult))
                for j in range(4):
                    o(dve.tensor_scalar(a[:, j], a[:, j], colv("rw_r_k", 1, j), None, ALU.mult))
                dve.sem_inc(ready.sem, ready.tick())
                dve.wait_ge(ready.sem, ready.at(3))
                five = lambda v_: v_.rearrange("p j (c s) -> p j c s", c=NCH)
                o(dve.tensor_tensor(kf, k, ei, ALU.mult))
                o(dve.tensor_tensor(bf, bf, ei, ALU.mult))
                o(dve.tensor_copy(last, five(el)[:, :, :, 63]))
                for j in range(4):
                    o(dve.tensor_tensor(kr[:, j, :, 0], five(kk)[:, j], five(tmp)[:, j], ALU.mult))
                    o(dve.tensor_tensor(kr[:, j, :, 1], five(r)[:, j], five(el)[:, j], ALU.mult))
                for q in range(2):
                    rows = slice(64 * q, 64 * q + 64)
                    o(dve.tensor_copy(kz[rows, q:8:2], kf[rows]))
                    o(dve.tensor_copy(bz[rows, q:8:2], bf[rows]))
                for j in range(4):
                    ends = last[:, j, :, None].to_broadcast([P, NCH, 64])
                    o(dve.tensor_tensor(five(kf)[:, j], five(kf)[:, j], ends, ALU.mult))
                    o(dve.tensor_tensor(five(bf)[:, j], five(bf)[:, j], ends, ALU.mult))
                for j in range(4):
                    dve.wait_ge(summed.sem, summed.at(j + 1))
                    dve.tensor_tensor(bonus[:, j], bank[j][:, 0:T], v[:, j], ALU.mult)

            @block.scalar
            def _(act):
                act.wait_ge(ready.sem, ready.at(1))
                act.activation(el, cum, ACT.Exp).then_inc(act_own.sem, act_own.tick())
                act.activation(ei, cum, ACT.Exp, scale=-1.0).then_inc(act_own.sem, act_own.tick())
                act.wait_ge(act_own.sem, act_own.total)
                act.wait_ge(ready.sem, ready.at(2))
                act.activation(tmp, tmp, ACT.Exp).then_inc(ready.sem, ready.tick())

            @block.tensor
            def _(pe):
                pe.wait_ge(ready.sem, ready.at(2))
                for j in range(4):
                    pe.matmul(bank[j][:, 0:T], half_ones[:], a[:, j], start=True, stop=True)\
                      .then_inc(summed.sem, summed.tick())

            end_phase()
            masks = scratch[:, SCRATCH - 12 * 64:].rearrange("p (a b) -> p a b", a=12)
            load_const(masks[0:64], "c_chunk_masks")
            consts_in = sig("consts_in")

            @block.tensor
            def _(pe):
                for n in range(3 * NCH):
                    src, cc = (kf, bf, v)[n // NCH], n % NCH
                    if n >= 4:
                        pe.wait_ge(copied.sem, copied.at(n - 3))
                    for j in range(4):
                        mm = pe.transpose(bank[n % 4][0:64, j * P:(j + 1) * P], src[:, j, cc * 64:cc * 64 + 64], ident[:])
                    mm.then_inc(turned.sem, turned.tick())

            @block.scalar
            def _(act):
                for n in range(3 * NCH):
                    act.wait_ge(turned.sem, turned.at(n + 1))
                    act.activation((kct, bct, vt)[n // NCH][0:64, n % NCH], bank[n % 4][0:64, :], ACT.Copy,
                                   scale=-1.0 if n // NCH == 1 else 1.0).then_inc(copied.sem, copied.tick())
                act.wait_ge(consts_in.sem, consts_in.total)

            end_phase()
            release(zone)
            br, ar = take(NCH, 8, P), take(NCH, 8, P)
            xt = take(NCH, 8, 64)
            state = take(4, P)
            wu = take(2, RW)
            ot = take(4, T)
            st = take(4, 64)
            assert used[0] <= SCRATCH - 12 * 64
            made, masked = sig("rw_made"), sig("rw_masked")
            top = slice(0, 64)

            @block.tensor
            def _(pe):
                for cc in range(NCH):
                    for i, z in enumerate((kz, bz)):
                        for hh in range(2):
                            n = cc * 4 + i * 2 + hh
                            if n >= 8:
                                pe.wait_ge(masked.sem, masked.at(n - 7))
                            for q in range(4):
                                hd = hh * 4 + q
                                mm = pe.matmul(bank[n % 8][top, q * P:(q + 1) * P], z[:, hd, cc * 64:cc * 64 + 64],
                                               kr[:, hd // 2, cc].rearrange("p a b -> p (a b)"), start=True, stop=True)
                            mm.then_inc(made.sem, made.tick())

            @block.vector
            def _(dve):
                for n in range(4 * NCH):
                    cc, i, hh = n // 4, n // 2 % 2, n % 2
                    dve.wait_ge(made.sem, made.at(n + 1))
                    mk_ = masks[top, 2 * i:2 * i + 2].rearrange("p a b -> p (a b)")[:, None, :].to_broadcast([64, 4, P])
                    dve.tensor_tensor((br, ar)[i][top, cc, 4 * hh:4 * hh + 4],
                                      bank[n % 8][top, :].rearrange("p (a b) -> p a b", a=4), mk_, ALU.mult)\
                       .then_inc(masked.sem, masked.tick())

            end_phase()
            xx = scratch[:, pads:pads + NCH * 512].rearrange("p (c h s) -> p c h s", c=NCH, h=8)
            am = scratch[:, pads + 2048:pads + 3072].rearrange("p (a h s) -> p a h s", a=2, h=8)
            pp = scratch[:, pads + 3072:pads + 4096].rearrange("p (a h s) -> p a h s", a=2, h=8)
            seeded, turned2, x_ready = sig("rw_seeded"), sig("turned"), sig("rw_x_ready")
            am_ready, p_made, p_ready, q_made = sig("rw_am_ready"), sig("rw_p_made"), sig("rw_p_ready"), sig("rw_q_made")

            def mask(i):
                return masks[top, i:i + 1].to_broadcast([64, 8, 64])

            @block.vector
            def _(dve):
                for cc in range(NCH):
                    ordered(dve, dve_own, dve.tensor_tensor(xt[top, cc], ar[top, cc, :, 0:64], mask(5), ALU.mult))
                    dve.tensor_tensor(xt[top, cc], xt[top, cc], mask(11), ALU.add).then_inc(seeded.sem, seeded.tick())
                for n in range(5 * NCH + 2):
                    if n < 5 * NCH:
                        lv, cc = divmod(n, NCH)
                        if n >= 2:
                            dve.wait_ge(p_made.sem, p_made.at(n - 1))
                        dve.tensor_tensor(am[top, n % 2], ar[top, cc, :, 0:64], mask(6 + lv), ALU.mult)\
                           .then_inc(am_ready.sem, am_ready.tick())
                    if n >= 2:
                        k_ = n - 2
                        lv, cc = divmod(k_, NCH)
                        dve.wait_ge(q_made.sem, q_made.at(k_ + 1))
                        for dst, b in ((xx[top, cc], bank[2 + k_ % 2]), (xt[top, cc], bank[4 + k_ % 2])):
                            i_ = dve.tensor_tensor(dst, dst, b[top, :].rearrange("p (h s) -> p h s", h=8), ALU.subtract)
                        i_.then_inc(x_ready.sem, x_ready.tick())

            @block.scalar
            def _(act):
                for cc in range(NCH):
                    act.wait_ge(turned2.sem, turned2.at(cc + 1))
                    act.activation(xx[top, cc], bank[6 + cc % 2][top, :].rearrange("p (h s) -> p h s", h=8), ACT.Copy)\
                       .then_inc(p_ready.sem, p_ready.tick())
                for n in range(5 * NCH):
                    act.wait_ge(p_made.sem, p_made.at(n + 1))
                    if n >= 2:
                        act.wait_ge(q_made.sem, q_made.at(n - 1))
                    act.activation(pp[top, n % 2], bank[n % 2][top, :].rearrange("p (h s) -> p h s", h=8), ACT.Copy)\
                       .then_inc(p_ready.sem, p_ready.tick())

            @block.tensor
            def _(pe):
                for cc in range(NCH):
                    pe.wait_ge(seeded.sem, seeded.at(cc + 1))
                    if cc >= 2:
                        pe.wait_ge(p_ready.sem, p_ready.at(cc - 1))
                    for hd in range(8):
                        mm = pe.transpose(bank[6 + cc % 2][top, hd * 64:hd * 64 + 64], xt[top, cc, hd], ident[0:64, 0:64])
                    mm.then_inc(turned2.sem, turned2.tick())
                for n in range(5 * NCH + 1):
                    if n < 5 * NCH:
                        lv, cc = divmod(n, NCH)
                        pe.wait_ge(am_ready.sem, am_ready.at(n + 1))
                        pe.wait_ge(p_ready.sem, p_ready.at(NCH if n < NCH else NCH + n - 1))
                        if n >= NCH:
                            pe.wait_ge(x_ready.sem, x_ready.at(n - NCH + 1))
                        for hd in range(8):
                            mm = pe.matmul(bank[n % 2][top, hd * 64:hd * 64 + 64], am[top, n % 2, hd], xx[top, cc, hd],
                                           start=True, stop=True)
                        mm.then_inc(p_made.sem, p_made.tick())
                    if n >= 1:
                        k_ = n - 1
                        lv, cc = divmod(k_, NCH)
                        pe.wait_ge(p_ready.sem, p_ready.at(NCH + k_ + 1))
                        if k_ >= 2:
                            pe.wait_ge(x_ready.sem, x_ready.at(k_ - 1))
                        for hd in range(8):
                            s = slice(hd * 64, hd * 64 + 64)
                            pe.matmul(bank[2 + k_ % 2][top, s], xt[top, cc, hd], pp[top, k_ % 2, hd], start=True, stop=True)
                            mm = pe.matmul(bank[4 + k_ % 2][top, s], pp[top, k_ % 2, hd], xt[top, cc, hd], start=True, stop=True)
                        mm.then_inc(q_made.sem, q_made.tick())

            end_phase()
            w_made, w_ready, u_made, u_ready = sig("rw_w_made"), sig("rw_w_ready"), sig("rw_u_made"), sig("rw_u_ready")
            o_made, o_ready, s_made, s_ready = sig("rw_o_made"), sig("rw_o_ready"), sig("rw_s_made"), sig("rw_s_ready")

            @block.gpsimd
            def _(pool):
                pool.memset(state, 0.0).then_inc(s_ready.sem, s_ready.tick())

            @block.tensor
            def _(pe):
                for cc in range(NCH):
                    pe.wait_ge(s_ready.sem, s_ready.at(cc + 1))
                    for hd in range(8):
                        j, s, half = hd // 2, slice(hd * 64, hd * 64 + 64), slice(hd % 2 * 64, hd % 2 * 64 + 64)
                        pe.matmul(bank[0][top, s], kr[:, j, cc, 0], state[:, j, half], start=True, stop=False)
                        mm = pe.matmul(bank[0][top, s], br[top, cc, hd, 0:64], vt[top, cc, s], start=False, stop=True)
                    mm.then_inc(w_made.sem, w_made.tick())
                    pe.wait_ge(w_ready.sem, w_ready.at(cc + 1))
                    for hd in range(8):
                        s = slice(hd * 64, hd * 64 + 64)
                        mm = pe.matmul(bank[1][top, s], xt[top, cc, hd], wu[top, 0, s], start=True, stop=True)
                    mm.then_inc(u_made.sem, u_made.tick())
                    pe.wait_ge(u_ready.sem, u_ready.at(cc + 1))
                    for hd in range(8):
                        j, s = hd // 2, slice(hd * 64, hd * 64 + 64)
                        pe.matmul(bank[3][:, s], kct[top, cc, j * P:(j + 1) * P], vt[top, cc, s], start=True, stop=False)
                        mm = pe.matmul(bank[3][:, s], bct[top, cc, j * P:(j + 1) * P], wu[top, 1, s], start=False, stop=True)
                    mm.then_inc(s_made.sem, s_made.tick())
                    if cc >= 1:
                        pe.wait_ge(o_ready.sem, o_ready.at(cc))
                    for hd in range(8):
                        j, s, half = hd // 2, slice(hd * 64, hd * 64 + 64), slice(hd % 2 * 64, hd % 2 * 64 + 64)
                        b = bank[2][half, j * 64:j * 64 + 64]
                        pe.matmul(b, state[:, j, half], kr[:, j, cc, 1], start=True, stop=False)
                        pe.matmul(b, vt[top, cc, s], br[top, cc, hd, 64:P], start=False, stop=False)
                        mm = pe.matmul(b, wu[top, 1, s], ar[top, cc, hd, 64:P], start=False, stop=True)
                    mm.then_inc(o_made.sem, o_made.tick())

            @block.scalar
            def _(act):
                for cc in range(NCH):
                    act.wait_ge(w_made.sem, w_made.at(cc + 1))
                    act.activation(wu[top, 0], bank[0][top, :], ACT.Copy).then_inc(w_ready.sem, w_ready.tick())
                    act.wait_ge(u_made.sem, u_made.at(cc + 1))
                    if cc >= 1:
                        act.wait_ge(o_made.sem, o_made.at(cc))
                    act.activation(wu[top, 1], bank[1][top, :], ACT.Copy).then_inc(u_ready.sem, u_ready.tick())
                    act.wait_ge(o_made.sem, o_made.at(cc + 1))
                    act.activation(ot[:, :, cc * 64:cc * 64 + 64], bank[2][:, 0:T].rearrange("p (j s) -> p j s", j=4),
                                   ACT.Copy).then_inc(o_ready.sem, o_ready.tick())

            @block.vector
            def _(dve):
                for cc in range(NCH):
                    dve.wait_ge(s_made.sem, s_made.at(cc + 1))
                    dve.wait_ge(o_made.sem, o_made.at(cc + 1))
                    for q in range(2):
                        rows = slice(64 * q, 64 * q + 64)
                        old = state[rows, :, 64 * q:64 * q + 64]
                        ordered(dve, dve_own, dve.tensor_tensor(
                            st[rows], old, last[rows, :, cc:cc + 1].to_broadcast([64, 4, 64]), ALU.mult))
                        i_ = dve.tensor_tensor(
                            old, st[rows], bank[3][rows, :].rearrange("p (j two s) -> p j two s", j=4, two=2)[:, :, q],
                            ALU.add)
                        if q:
                            i_.then_inc(s_ready.sem, s_ready.tick())
                            dve.wait_ge(s_ready.sem, s_ready.at(cc + 2))

            end_phase()
            centered = sig("rw_centered")

            @block.tensor
            def _(pe):
                for j in range(4):
                    pe.matmul(bank[j][:, 0:T], half_ones[:], ot[:, j], start=True, stop=True)\
                      .then_inc(summed.sem, summed.tick())

            @block.vector
            def _(dve):
                for j in range(4):
                    dve.wait_ge(summed.sem, summed.at(j + 1))
                    dve.scalar_tensor_tensor(out=ot[:, j], in0=bank[j][:, 0:T], scalar=-1.0 / 64, in1=ot[:, j],
                                             op0=ALU.mult, op1=ALU.add)

            end_phase()
            norm(ot, [[j] for j in range(4)], 64, lambda t: colv("rw_ln_w", 1, t), ot, summer=half_ones[:], eps=GN_COL)

            @block.vector
            def _(dve):
                for j in range(4):
                    ordered(dve, dve_own, dve.scalar_tensor_tensor(out=ot[:, j], in0=ot[:, j], scalar=colv("rw_ln_b", 1, j),
                                                                   in1=bonus[:, j], op0=ALU.add, op1=ALU.add))
                dve.tensor_tensor(ya, ot, g, ALU.mult)

            end_phase()
            release(mark)

        moe_loop = {}

        def moe():
            E = N_EXPERTS
            mark = used[0]
            x, xt = take(DT, T), take(TT, D)
            slots, before = take(T), take(P)
            wr, lg, row_b = take(DT, E), take(TT, E), take(E)
            eq, one, two, two_l = (take(TT, E) for _ in range(4))
            pick, gates, place = take(TT, E), take(TT, E), take(TT, E)
            count, crowd = take(E), take(E)
            top = take(8, TT)
            norm_model(h, "norm_ffn", 1, x)
            consts_in = sig("consts_in")
            load_const(slots, "c_slots")
            load_const(before, "c_before")
            load_const(wr, "router_view")
            load_const(row_b[0:1], "moe_b_router")
            turned, copied, routed, chosen, placed = (sig(n) for n in ("turned", "copied", "routed", "chosen", "placed"))

            @block.tensor
            def _(pe):
                pe.wait_ge(consts_in.sem, consts_in.total)
                for t in range(TT):
                    for k in range(DT):
                        pe.matmul(bank[4 + t][:, 0:E], x[:, k, t * P:(t + 1) * P], wr[:, k], start=k == 0, stop=False)
                    pe.matmul(bank[4 + t][:, 0:E], ones[0:1, :], row_b[0:1, :], start=False, stop=True)\
                      .then_inc(routed.sem, routed.tick())
                for n in range(4):
                    t, half = divmod(n, 2)
                    for m in range(4):
                        mm = pe.transpose(bank[n][:, m * P:(m + 1) * P], x[:, 4 * half + m, t * P:(t + 1) * P], ident[:])
                    mm.then_inc(turned.sem, turned.tick())
                pe.wait_ge(chosen.sem, chosen.at(1))
                pe.wait_ge(copied.sem, copied.at(4))
                pe.matmul(bank[6][:, 0:E], before, pick[:, 0], start=True, stop=True)
                pe.matmul(bank[7][:, 0:E], ones[:], pick[:, 0], start=True, stop=False)
                pe.matmul(bank[7][:, 0:E], before, pick[:, 1], start=False, stop=True)
                for t in range(TT):
                    mm = pe.matmul(bank[0][:, 0:E], ones[:], pick[:, t], start=t == 0, stop=t == TT - 1)
                mm.then_inc(placed.sem, placed.tick())

            @block.scalar
            def _(act):
                act.wait_ge(consts_in.sem, consts_in.total)
                for n in range(4):
                    t, half = divmod(n, 2)
                    act.wait_ge(turned.sem, turned.at(n + 1))
                    act.activation(xt[:, t, half * 512:(half + 1) * 512], bank[n][:, :], ACT.Copy)\
                       .then_inc(copied.sem, copied.tick())
                act.wait_ge(chosen.sem, chosen.at(1))
                act.activation(top[:, 3], top[:, 2], ACT.Exp).then_inc(chosen.sem, chosen.tick())

            @block.vector
            def _(dve):
                def o(i_):
                    ordered(dve, dve_own, i_)

                def wide(v_):
                    return v_[:, :, None].to_broadcast([P, TT, E])

                def first_of(hit, src, dst):
                    o(dve.tensor_tensor(eq, src, wide(hit), ALU.is_equal))
                    for t in range(TT):
                        o(dve.tensor_tensor_scan(two_l[:, t], ones[:, 0:E], eq[:, t], 0.0, ALU.mult, ALU.add))
                    o(dve.scalar_tensor_tensor(out=dst, in0=two_l, scalar=1.0, in1=eq, op0=ALU.is_le, op1=ALU.mult))

                for t in range(TT):
                    dve.wait_ge(routed.sem, routed.at(t + 1))
                    o(dve.tensor_copy(lg[:, t], bank[4 + t][:, 0:E]))
                o(dve.tensor_reduce(top[:, 0], lg, AX_X, ALU.max))
                first_of(top[:, 0], lg, one)
                o(dve.scalar_tensor_tensor(out=lg, in0=one, scalar=MASKED, in1=lg, op0=ALU.mult, op1=ALU.add))
                o(dve.tensor_reduce(top[:, 1], lg, AX_X, ALU.max))
                first_of(top[:, 1], lg, two)
                o(dve.tensor_tensor(top[:, 2], top[:, 1], top[:, 0], ALU.subtract))
                dve.tensor_tensor(pick, one, two, ALU.add).then_inc(chosen.sem, chosen.tick())
                dve.wait_ge(chosen.sem, chosen.at(2))
                o(dve.tensor_scalar(top[:, 4], top[:, 3], 1.0, None, ALU.add))
                o(dve.reciprocal(top[:, 5], top[:, 4]))
                o(dve.tensor_tensor(top[:, 6], top[:, 3], top[:, 5], ALU.mult))
                o(dve.tensor_tensor(gates, one, wide(top[:, 5]), ALU.mult))
                o(dve.tensor_tensor(two, two, wide(top[:, 6]), ALU.mult))
                o(dve.tensor_tensor(gates, gates, two, ALU.add))
                dve.wait_ge(placed.sem, placed.at(1))
                for t in range(TT):
                    dve.tensor_copy(place[:, t], bank[6 + t][:, 0:E])
                o(dve.tensor_scalar(count, bank[0][:, 0:E], float(CROWD), None, ALU.is_gt))
                dve.tensor_copy(crowd.bitcast(mybir.dt.int32), count)

            end_phase()

            to_slot, to_token = take(TT, T), take(TT, T)
            xg, gt = take(DT, T), take(TT, T)
            sg, acts, ye = take(2, T), take(ET, T), take(TT, D)
            pos[0] += -pos[0] % RING
            first_pos = pos[0]
            use0 = list(slot_use)
            srcs = []
            wg = ins["moe_w_gate"][0].rearrange("e (k p) n -> p e k n", p=P)
            wu = ins["moe_w_up"][0].rearrange("e (k p) n -> p e k n", p=P)
            wd = ins["moe_w_down"][0].rearrange("e (k p) n -> p e k n", p=P)
            for a in range(0, D_FE, 256):
                srcs.append(lambda e, a=a: wg[:, e, :, a:a + 256])
                srcs.append(lambda e, a=a: wu[:, e, :, a:a + 256])
            for k in range(0, ET, 2):
                srcs.append(lambda e, k=k: wd[:, e, k:k + 2, :])
            NC = len(srcs)
            assert NC % RING == 0
            per_slot = NC // RING
            views = [ring[:, m % RING, :].rearrange("p (a b) -> p a b", a=8 if m < 2 * (ET // 2) else 2)
                     for m in range(NC)]
            rel = [0] * NC
            base = tiles_done.total
            PER = 2 * ET + ET // 2
            for m in range(0, ET, 2):
                rel[m], rel[m + 1] = 2 * m + 3, 2 * m + 4
            for m in range(ET, NC):
                rel[m] = 2 * ET + (m - ET) + 1
            multiplied_own = sig("moe_slots_made")
            gathered, fetched, one_hot, gate_in, gate_out = (
                sig(n) for n in ("moe_gathered", "moe_fetched", "moe_one_hot", "moe_gate_turned", "moe_gate_copied"))
            gated, multiplied, y_out, mixed, added = (
                sig(n) for n in ("gated", "multiplied", "moe_y_copied", "moe_mixed", "moe_added"))
            per = {gathered: 8, fetched: 8, one_hot: 1, gate_in: 1, gate_out: 1, gated: ET, multiplied: ET,
                   y_out: 1, mixed: 4, added: 4, tiles_done: PER}

            def wait(eng, s_, e, n):
                eng.wait_ge(s_.sem, e * per[s_] + (s_.base + n))

            def chunk_in(pe, e, m):
                s_ = m % RING
                pe.wait_ge(landed[s_].sem, e * (16 * per_slot) + 16 * (use0[s_] + m // RING + 1))

            def crowded(eng, e):
                return eng.value_load(crowd[0:1, bass.ds(e, 1)].bitcast(mybir.dt.int32), min_val=0, max_val=1)

            def expert_products(pe, e, W):
                ST = W // P
                for m in range(DT):
                    if m >= 4:
                        wait(pe, fetched, e, m - 3)
                    for t in range(TT):
                        mm = pe.matmul(bank[m % 4][:, 0:W], xt[:, t, m * P:(m + 1) * P], to_slot[:, t, 0:W],
                                       start=t == 0, stop=t == TT - 1)
                    mm.then_inc(gathered.sem, 1)
                for s_ in range(ST):
                    for t in range(TT):
                        mm = pe.transpose(bank[4][:, s_ * T + t * P:s_ * T + (t + 1) * P],
                                          to_token[:, t, s_ * P:(s_ + 1) * P], ident[:])
                mm.then_inc(gate_in.sem, 1)
                wait(pe, fetched, e, DT)
                for i in range(ET):
                    if i >= 2:
                        wait(pe, multiplied, e, i - 1)
                    for q in range(2):
                        m = i // 2 * 2 + q
                        if i % 2 == 0:
                            chunk_in(pe, e, m)
                        for k in range(DT):
                            mm = pe.matmul(bank[2 * i % 4 + q][:, 0:W], views[m][:, k, i % 2 * P:(i % 2 + 1) * P],
                                           xg[:, k, 0:W], start=k == 0, stop=k == DT - 1)
                        mm.then_inc(tiles_done.sem, 1)
                wait(pe, gate_out, e, 1)
                for i in range(ET // 2):
                    m = ET + i
                    wait(pe, multiplied, e, 2 * i + 2)
                    chunk_in(pe, e, m)
                    for kk in range(2):
                        k = 2 * i + kk
                        for s_ in range(ST):
                            for half in range(2):
                                mm = pe.matmul(bank[4 + 2 * s_ + half][:, :], acts[:, k, s_ * P:(s_ + 1) * P],
                                               views[m][:, kk, half * 512:(half + 1) * 512], start=k == 0,
                                               stop=k == ET - 1)
                    mm.then_inc(tiles_done.sem, 1)
                wait(pe, y_out, e, 1)
                for b in range(4):
                    for q in range(2):
                        m = 2 * b + q
                        for s_ in range(ST):
                            mm = pe.matmul(bank[b][:, q * T:(q + 1) * T], ye[:, s_, m * P:(m + 1) * P], gt[:, s_],
                                           start=s_ == 0, stop=s_ == ST - 1)
                    mm.then_inc(mixed.sem, 1)

            @block.tensor
            def _(pe):
                with pe.Fori(0, E) as e:
                    wait(pe, one_hot, e, 1)
                    many = crowded(pe, e)
                    with pe.If(many == 1):
                        expert_products(pe, e, T)
                    with pe.Else():
                        expert_products(pe, e, P)

            def expert_copies(act, e, W):
                ST = W // P
                for m in range(DT):
                    wait(act, gathered, e, m + 1)
                    act.activation(xg[:, m, 0:W], bank[m % 4][:, 0:W], ACT.Copy).then_inc(fetched.sem, 1)
                wait(act, gate_in, e, 1)
                act.activation(gt[:, 0:ST], bank[4][:, 0:ST * T].rearrange("p (a b) -> p a b", b=T), ACT.Copy)\
                   .then_inc(gate_out.sem, 1)
                for i in range(ET):
                    wait(act, tiles_done, e, 2 * i + 1)
                    if i >= 2:
                        wait(act, multiplied, e, i - 1)
                    act.activation(sg[:, i % 2, 0:W], bank[2 * i % 4][:, 0:W], ACT.Silu).then_inc(gated.sem, 1)
                wait(act, tiles_done, e, PER)
                for s_ in range(ST):
                    for half in range(2):
                        last_ = act.activation(ye[:, s_, half * 512:(half + 1) * 512], bank[4 + 2 * s_ + half][:, :],
                                               ACT.Copy)
                last_.then_inc(y_out.sem, 1)

            @block.scalar
            def _(act):
                with act.Fori(0, E) as e:
                    many = crowded(act, e)
                    with act.If(many == 1):
                        expert_copies(act, e, T)
                    with act.Else():
                        expert_copies(act, e, P)

            def expert_products_of_gates(dve, e, W):
                for i in range(ET):
                    wait(dve, tiles_done, e, 2 * i + 2)
                    wait(dve, gated, e, i + 1)
                    dve.tensor_tensor(acts[:, i, 0:W], bank[2 * i % 4 + 1][:, 0:W], sg[:, i % 2, 0:W], ALU.mult)\
                       .then_inc(multiplied.sem, 1)

            @block.vector
            def _(dve):
                with dve.Fori(0, E) as e:
                    for t in range(TT):
                        dve.tensor_scalar(to_slot[:, t], slots, place[:, t, bass.ds(e, 1)], pick[:, t, bass.ds(e, 1)],
                                          ALU.is_equal, ALU.mult).then_inc(multiplied_own.sem, 1)
                    dve.wait_ge(multiplied_own.sem, e * 2 + (multiplied_own.base + 2))
                    for t in range(TT):
                        i_ = dve.tensor_scalar(to_token[:, t], to_slot[:, t], gates[:, t, bass.ds(e, 1)], None, ALU.mult)
                    i_.then_inc(one_hot.sem, 1)
                    many = crowded(dve, e)
                    with dve.If(many == 1):
                        expert_products_of_gates(dve, e, T)
                    with dve.Else():
                        expert_products_of_gates(dve, e, P)
                    for b in range(4):
                        wait(dve, mixed, e, b + 1)
                        dve.tensor_tensor(h[:, 2 * b:2 * b + 2], bank[b][:, :].rearrange("p (a b) -> p a b", a=2),
                                          h[:, 2 * b:2 * b + 2], ALU.add).then_inc(added.sem, 1)
                    wait(dve, added, e, 4)

            per[multiplied_own] = 2
            for s_, n in per.items():
                s_.tick(E * n)

            def load(sp, e, m, value):
                if value is not None:
                    sp.wait_ge(tiles_done.sem, value)
                sp.dma_start(views[m], srcs[m](e)).then_inc(landed[m % RING].sem, 16)

            def loads(sp, last):
                for m in range(RING):
                    load(sp, 0, m, last[m])
                with sp.Fori(2, E + 1) as count:
                    e = count - 2
                    for m in range(RING, NC):
                        ahead = m + (m == ET - 1)
                        load(sp, e, m, None if m == ET else e * PER + (base + rel[ahead - RING]))
                    for m in range(RING):
                        load(sp, e + 1, m, e * PER + (base + rel[NC - RING + m]))
                for m in range(RING, NC):
                    load(sp, E - 1, m, (E - 1) * PER + base + rel[m - RING])
                for m in range(NC - RING, NC):
                    last[m % RING] = (E - 1) * PER + base + rel[m]

            plan.append(loads)
            for s_ in range(RING):
                slot_use[s_] += E * per_slot
            pos[0] += E * NC
            end_phase()
            release(mark)
        stages = []
        setup()
        import_stages = [lambda: layer0_mixer(), lambda: cross_attention(0), lambda: swiglu(),
                         lambda: diff_mixer(), lambda: cross_attention(1), lambda: moe(),
                         lambda: hybrid(0), lambda: conv_ffn(0), lambda: hybrid(1), lambda: conv_ffn(1)]
        for n in (range(len(import_stages)) if stop is None else stop):
            import_stages[n]()
        finish()

        @block.sync
        def _(sp):
            last = [None] * RING
            for c in plan:
                if callable(c):
                    c(sp, last)
                    continue
                if last[c.slot] is not None:
                    sp.wait_ge(tiles_done.sem, last[c.slot])
                sp.dma_start(c.dst, c.src).then_inc(landed[c.slot].sem, 16)
                last[c.slot] = c.release


NAMES = """x mem norm_mix norm_xattn norm_mem norm_ffn xa_w_q xa_w_kv xa_q_gain xa_k_gain xa_w_o hy_w_in rw_mu rw_w0
rw_w_up rw_a0 rw_a_up rw_g_up rw_k_k rw_k_a rw_r_k rw_ln_w rw_ln_b s5_lam_re s5_lam_im s5_log_dt s5_b_re s5_b_im
s5_c_re s5_c_im s5_d s5_w_glu s5_b_glu hy_w_out ff_w_gate ff_w_up ff_w_down da_w_qkv da_q_gain da_k_gain da_lam_q1
da_lam_k1 da_lam_q2 da_lam_k2 da_sub_gain da_w_o moe_w_router moe_b_router moe_w_gate moe_w_up moe_w_down rel_bias_2
ln_mix_pre_2 ln_mix_post_2 ln_ffn_pre_2 ln_ffn_post_2 w_in_2 b_f_2 q_norm_2 kv_norm_2 w_uq_2 w_ukv_2 w_o_2 w_up_2
conv_w_2 conv_b_2 w_down_2""".split()


STOP = None


def kernel(**inputs):
    import concourse.bacc as bacc
    from concourse.bass_utils import run_bass_kernel_spmd

    nc = bacc.Bacc("TRN2", target_bir_lowering=False, num_devices=1)
    arrays, args = {}, {}
    given = [(n, np.ascontiguousarray(inputs[n])) for n in NAMES]
    given += [("c_" + n, np.ascontiguousarray(a)) for n, a in const_arrays().items()]
    for name, a in given:
        arrays[f"in_{name}"] = a
        args[name] = nc.dram_tensor(f"in_{name}", a.shape, mybir.dt.from_np(a.dtype), kind="ExternalInput").ap()
    args["router_view"] = args["moe_w_router"][0].rearrange("(k p) n -> p k n", p=P)
    out = nc.dram_tensor("out_0", (1, T, D), F32, kind="ExternalOutput").ap()
    build(nc, args, out, STOP)
    r = run_bass_kernel_spmd(nc, [arrays], core_ids=[0])
    return r.results[0]["out_0"]
```
